# Optimizing a Trainium2 kernel written in Bass

```python
import math
import jax, jax.numpy as jnp
from jax import lax
import numpy as np

D_MODEL = 1024
BATCH = 1
SEQ = 512
DEPTH = 2

N_EVEN = (DEPTH + 1) // 2
N_ODD = DEPTH // 2
HEAD_DIM = 64
MIX_HALF = D_MODEL // 2
ROPE_DIM = HEAD_DIM // 4
ROPE_THETA = 500000.0
EPS = 1e-6
NEG_INF = -1e30

NSA_HEADS = MIX_HALF // HEAD_DIM
NSA_KV_HEADS = max(1, NSA_HEADS // 4)
NSA_GROUP = NSA_HEADS // NSA_KV_HEADS
CMP_BLOCK = 32
CMP_STRIDE = 16
CMP_HIDDEN = 256
SLC_BLOCK = 64
SLC_TOPK = 16
WINDOW = 512
Q_BLOCK = 128
FORCE_SCORE = 1e3

GMLP_GROUPS = MIX_HALF // HEAD_DIM
GMLP_CHUNK = 128

RWKV_HEADS = MIX_HALF // HEAD_DIM
DECAY_LORA = 64
ICLR_LORA = 64
GATE_LORA = 128

LRU_WIDTH = MIX_HALF
LRU_BLOCKS = 8
LRU_CONV = 4
LRU_C = 8.0

D_FF = 11 * D_MODEL // 4
FFN_CONV = 3

NSA_Q = NSA_HEADS * HEAD_DIM
NSA_KV = NSA_KV_HEADS * HEAD_DIM
EVEN_SIZES = (NSA_Q,) + (NSA_KV,) * 6 + (3 * NSA_HEADS, MIX_HALF, MIX_HALF)
EVEN_COLS = sum(EVEN_SIZES)
RWKV_SIZES = (MIX_HALF, MIX_HALF, MIX_HALF, DECAY_LORA, ICLR_LORA, GATE_LORA)
RWKV_COLS = sum(RWKV_SIZES)
ODD_COLS = RWKV_COLS + 2 * LRU_WIDTH

kernel_name = 'hybrid_nsa_gmlp_rwkv7_rglru_block'

def rms_norm(x, g):
    xf = x.astype(jnp.float32)
    y = xf * lax.rsqrt(jnp.mean(xf * xf, axis=-1, keepdims=True) + EPS)
    return (y * g.astype(jnp.float32)).astype(x.dtype)

def layer_norm(x, g, b):
    xf = x.astype(jnp.float32)
    mu = jnp.mean(xf, axis=-1, keepdims=True)
    var = jnp.mean(jnp.square(xf - mu), axis=-1, keepdims=True)
    y = (xf - mu) * lax.rsqrt(var + EPS) * g.astype(jnp.float32) + b.astype(jnp.float32)
    return y.astype(x.dtype)

def modulate(h, shift, scale):
    return h * (1 + scale[:, None, :]) + shift[:, None, :]

def split_cols(p, sizes):
    offs = np.cumsum(sizes)[:-1].tolist()
    return jnp.split(p, offs, axis=-1)

def token_shift(z):
    return jnp.pad(z, ((0, 0), (1, 0), (0, 0)))[:, :-1]

def causal_dwconv(x, w, b):
    K, C = w.shape
    y = lax.conv_general_dilated(x, w[:, None, :].astype(x.dtype), window_strides=(1,),
                                 padding=[(K - 1, 0)], dimension_numbers=('NWC', 'WIO', 'NWC'),
                                 feature_group_count=C)
    return y + b.astype(x.dtype)

def rope_tables(positions):
    inv = ROPE_THETA ** (-jnp.arange(0, ROPE_DIM, 2, dtype=jnp.float32) / ROPE_DIM)
    ang = positions.astype(jnp.float32)[..., None] * inv
    return jnp.cos(ang), jnp.sin(ang)

def apply_rope(x, cos, sin):
    half = ROPE_DIM // 2
    xf = x.astype(jnp.float32)
    x1, x2, rest = xf[..., :half], xf[..., half:ROPE_DIM], xf[..., ROPE_DIM:]
    c, s = cos[:, :, None, :], sin[:, :, None, :]
    return jnp.concatenate([x1 * c - x2 * s, x2 * c + x1 * s, rest], axis=-1).astype(x.dtype)

def masked_softmax(s, mask):
    return jax.nn.softmax(jnp.where(mask, s.astype(jnp.float32), NEG_INF), axis=-1)

def compress_blocks(k, tok, pe, w1, w2):
    B, _, Hk, hd = k.shape
    n_cmp, L = tok.shape
    blk = k[:, tok] + pe[:, None, :].astype(k.dtype)
    blk = jnp.swapaxes(blk, 2, 3).reshape(B, n_cmp, Hk, L * hd)
    return jax.nn.gelu(blk @ w1) @ w2

def nsa_attention(q, k_c, v_c, k_s, v_s, k_w, v_w, gate_logits, cos, sin,
                  pe_k, w1_k, w2_k, pe_v, w1_v, w2_v):
    B, T, _ = q.shape
    H, Hk, G, hd = NSA_HEADS, NSA_KV_HEADS, NSA_GROUP, HEAD_DIM
    scale = hd ** -0.5
    q = apply_rope(q.reshape(B, T, H, hd), cos, sin).reshape(B, T, Hk, G, hd)
    k_c, v_c, k_s, v_s, k_w, v_w = [z.reshape(B, T, Hk, hd) for z in (k_c, v_c, k_s, v_s, k_w, v_w)]
    k_s = apply_rope(k_s, cos, sin)
    k_w = apply_rope(k_w, cos, sin)
    t_idx = jnp.arange(T)

    n_cmp = (T - CMP_BLOCK) // CMP_STRIDE + 1
    cmp_start = jnp.arange(n_cmp) * CMP_STRIDE
    cmp_end = cmp_start + CMP_BLOCK - 1
    tok = cmp_start[:, None] + jnp.arange(CMP_BLOCK)[None, :]
    kcmp = compress_blocks(k_c, tok, pe_k, w1_k, w2_k)
    vcmp = compress_blocks(v_c, tok, pe_v, w1_v, w2_v)
    kcmp = apply_rope(kcmp, cos[:, cmp_end], sin[:, cmp_end])
    s_c = jnp.einsum('btkgd,bnkd->bkgtn', q, kcmp).astype(jnp.float32) * scale
    valid_c = cmp_end[None, :] <= t_idx[:, None]
    p_c = masked_softmax(s_c, valid_c) * valid_c
    o_c = jnp.einsum('bkgtn,bnkd->btkgd', p_c.astype(vcmp.dtype), vcmp)

    n_slc = T // SLC_BLOCK
    k_top = min(SLC_TOPK, n_slc)
    slc_start = jnp.arange(n_slc) * SLC_BLOCK
    overlap = jnp.clip(jnp.minimum(cmp_start[:, None] + CMP_BLOCK, slc_start[None, :] + SLC_BLOCK)
                       - jnp.maximum(cmp_start[:, None], slc_start[None, :]), 0).astype(jnp.float32) / CMP_BLOCK
    imp = jnp.einsum('bkgtn,nj->bktj', p_c, overlap)
    cur = t_idx // SLC_BLOCK
    j = jnp.arange(n_slc)
    forced = (j[None, :] == 0) | (j[None, :] == cur[:, None]) | (j[None, :] == cur[:, None] - 1)
    causal_s = slc_start[None, :] <= t_idx[:, None]
    score = jnp.where(forced, FORCE_SCORE, jnp.where(causal_s, imp, -1.0))
    _, sel = lax.top_k(score, k_top)

    nq = T // Q_BLOCK
    ks_blk = jnp.swapaxes(k_s, 1, 2).reshape(B, Hk, n_slc, SLC_BLOCK, hd)
    vs_blk = jnp.swapaxes(v_s, 1, 2).reshape(B, Hk, n_slc, SLC_BLOCK, hd)
    pad = ((0, 0), (0, 0), (WINDOW, 0), (0, 0))
    kw_pad = jnp.pad(jnp.swapaxes(k_w, 1, 2), pad)
    vw_pad = jnp.pad(jnp.swapaxes(v_w, 1, 2), pad)
    q_ch = q.reshape(B, nq, Q_BLOCK, Hk, G, hd).transpose(1, 0, 3, 4, 2, 5)
    sel_ch = sel.reshape(B, Hk, nq, Q_BLOCK, k_top).transpose(2, 0, 1, 3, 4)
    starts = jnp.arange(nq) * Q_BLOCK
    b_i = jnp.arange(B)[:, None, None, None]
    h_i = jnp.arange(Hk)[None, :, None, None]
    n_sel_keys = k_top * SLC_BLOCK

    def query_block(args):
        qb, selb, s0 = args
        tq = s0 + jnp.arange(Q_BLOCK)
        kg = ks_blk[b_i, h_i, selb].reshape(B, Hk, Q_BLOCK, n_sel_keys, hd)
        vg = vs_blk[b_i, h_i, selb].reshape(B, Hk, Q_BLOCK, n_sel_keys, hd)
        kpos = (selb[..., None] * SLC_BLOCK + jnp.arange(SLC_BLOCK)).reshape(B, Hk, Q_BLOCK, n_sel_keys)
        m_s = (kpos <= tq[:, None])[:, :, None]
        s_s = jnp.einsum('bkgqd,bkqnd->bkgqn', qb, kg).astype(jnp.float32) * scale
        p_s = masked_softmax(s_s, m_s)
        o_s = jnp.einsum('bkgqn,bkqnd->bkgqd', p_s.astype(vg.dtype), vg)
        kwb = lax.dynamic_slice_in_dim(kw_pad, s0, Q_BLOCK + WINDOW, axis=2)
        vwb = lax.dynamic_slice_in_dim(vw_pad, s0, Q_BLOCK + WINDOW, axis=2)
        kp = s0 - WINDOW + jnp.arange(Q_BLOCK + WINDOW)
        m_w = (kp[None, :] <= tq[:, None]) & (kp[None, :] > tq[:, None] - WINDOW) & (kp[None, :] >= 0)
        s_w = jnp.einsum('bkgqd,bknd->bkgqn', qb, kwb).astype(jnp.float32) * scale
        p_w = masked_softmax(s_w, m_w)
        o_w = jnp.einsum('bkgqn,bknd->bkgqd', p_w.astype(vwb.dtype), vwb)
        return o_s, o_w

    o_s, o_w = lax.map(query_block, (q_ch, sel_ch, starts))
    o_s = o_s.transpose(1, 0, 4, 2, 3, 5).reshape(B, T, Hk, G, hd)
    o_w = o_w.transpose(1, 0, 4, 2, 3, 5).reshape(B, T, Hk, G, hd)
    gate = jax.nn.sigmoid(gate_logits.astype(jnp.float32)).reshape(B, T, Hk, G, 3).astype(q.dtype)
    out = gate[..., 0:1] * o_c + gate[..., 1:2] * o_s + gate[..., 2:3] * o_w
    return out.reshape(B, T, H * hd)

def gmlp_spatial_gating(u, v, ln_g, ln_b, ws, bs):
    B, T, W = u.shape
    gw = W // GMLP_GROUPS
    u = jax.nn.gelu(u)
    v = layer_norm(jax.nn.gelu(v).reshape(B, T, GMLP_GROUPS, gw), ln_g, ln_b)
    v = v.reshape(B, T // GMLP_CHUNK, GMLP_CHUNK, GMLP_GROUPS, gw)
    causal = jnp.tril(jnp.ones((GMLP_CHUNK, GMLP_CHUNK), dtype=bool))
    w = jnp.where(causal, ws, 0)
    mixed = jnp.einsum('gts,bcsgd->bctgd', w.astype(v.dtype), v) + bs.T[:, :, None].astype(v.dtype)
    return u * mixed.reshape(B, T, W)

def even_mixer(h, cos, sin, w_in, w_out, pe_k, w1_k, w2_k, pe_v, w1_v, w2_v, ln_g, ln_b, ws, bs):
    q, k_c, v_c, k_s, v_s, k_w, v_w, gates, u, v = split_cols(h @ w_in, EVEN_SIZES)
    y_a = nsa_attention(q, k_c, v_c, k_s, v_s, k_w, v_w, gates, cos, sin, pe_k, w1_k, w2_k, pe_v, w1_v, w2_v)
    y_b = gmlp_spatial_gating(u, v, ln_g, ln_b, ws, bs)
    return jnp.concatenate([y_a, y_b], axis=-1) @ w_out

def rwkv7_time_mix(r, k, v, wl, al, gl, w0, wB, a0, aB, gB, xi, alpha, rho, ln_g, ln_b):
    B, T, _ = r.shape
    H, hd = RWKV_HEADS, HEAD_DIM
    f32 = jnp.float32
    log_w = -math.exp(-0.5) * jax.nn.sigmoid((w0 + jnp.tanh(wl) @ wB).astype(f32))
    a = jax.nn.sigmoid((a0 + al @ aB).astype(f32))
    g = jax.nn.sigmoid(gl) @ gB
    heads = lambda z: z.astype(f32).reshape(B, T, H, hd)
    r_, k_, v_, a_, w_ = heads(r), heads(k), heads(v), heads(a), jnp.exp(heads(log_w))
    kappa = k_ * xi.astype(f32).reshape(H, hd)
    kappa = kappa * lax.rsqrt(jnp.sum(kappa * kappa, axis=-1, keepdims=True) + EPS)
    kt = k_ * (1 + (a_ - 1) * alpha.astype(f32).reshape(H, hd))

    def step(S, inp):
        w_t, kh_t, a_t, kt_t, v_t, r_t = inp
        Sk = jnp.einsum('bhvk,bhk->bhv', S, kh_t)
        S = S * w_t[:, :, None, :] - Sk[..., None] * (a_t * kh_t)[:, :, None, :] + v_t[..., None] * kt_t[:, :, None, :]
        return S, jnp.einsum('bhvk,bhk->bhv', S, r_t)

    xs = tuple(jnp.moveaxis(z, 1, 0) for z in (w_, kappa, a_, kt, v_, r_))
    _, y = lax.scan(step, jnp.zeros((B, H, hd, hd), f32), xs)
    y = jnp.moveaxis(y, 0, 1)
    bonus = jnp.sum(r_ * rho.astype(f32).reshape(H, hd) * kt, axis=-1, keepdims=True) * v_
    out = layer_norm(y, ln_g, ln_b) + bonus
    return g * out.reshape(B, T, H * hd).astype(g.dtype)

def rglru_branch(gate_in, x_in, conv_w, conv_b, wa, ba, wx, bx, lam):
    B, T, W = x_in.shape
    f32 = jnp.float32
    xc = causal_dwconv(x_in, conv_w, conv_b)
    xb = xc.reshape(B, T, LRU_BLOCKS, W // LRU_BLOCKS)
    r = jax.nn.sigmoid((jnp.einsum('btnd,nde->btne', xb, wa).reshape(B, T, W) + ba).astype(f32))
    i = jax.nn.sigmoid((jnp.einsum('btnd,nde->btne', xb, wx).reshape(B, T, W) + bx).astype(f32))
    log_a = -LRU_C * r * jax.nn.softplus(-lam.astype(f32))
    a = jnp.exp(log_a)
    b = jnp.sqrt(-jnp.expm1(2 * log_a)) * (i * xc.astype(f32))

    def combine(left, right):
        a1, b1 = left
        a2, b2 = right
        return a1 * a2, a2 * b1 + b2

    _, hseq = lax.associative_scan(combine, (a, b), axis=1)
    return jax.nn.gelu(gate_in) * hseq.astype(gate_in.dtype)

def odd_mixer(h, w_in, w_out, mu, w0, wB, a0, aB, gB, xi, alpha, rho, ln_g, ln_b,
              conv_w, conv_b, wa, ba, wx, bx, lam):
    p = h @ w_in
    pc, pd = p[..., :RWKV_COLS], p[..., RWKV_COLS:]
    pc = pc + mu * (token_shift(pc) - pc)
    r, k, v, wl, al, gl = split_cols(pc, RWKV_SIZES)
    y_c = rwkv7_time_mix(r, k, v, wl, al, gl, w0, wB, a0, aB, gB, xi, alpha, rho, ln_g, ln_b)
    gate_d, x_d = jnp.split(pd, 2, axis=-1)
    y_d = rglru_branch(gate_d, x_d, conv_w, conv_b, wa, ba, wx, bx, lam)
    return jnp.concatenate([y_c, y_d], axis=-1) @ w_out

def conv_glu_ffn(h, w_up, conv_w, conv_b, w_down):
    up = causal_dwconv(h @ w_up, conv_w, conv_b)
    a, b = jnp.split(up, 2, axis=-1)
    return (jax.nn.silu(a) * b) @ w_down

def setup_inputs(seed: int = 0) -> dict:
    key = jax.random.key(seed)
    ks = iter(jax.random.split(key, 64))
    nrm = lambda shape, s: s * jax.random.normal(next(ks), shape, jnp.float32)
    D, NE, NO, F2 = D_MODEL, N_EVEN, N_ODD, 2 * D_FF
    gw = MIX_HALF // LRU_BLOCKS
    u = jax.random.uniform(next(ks), (NO, LRU_WIDTH), jnp.float32, 0.9, 0.999)
    a_base = u ** (1.0 / LRU_C)
    lam = jnp.log(a_base) - jnp.log1p(-a_base)
    return {
        'x': nrm((BATCH, SEQ, D), 1.0),
        'c': nrm((BATCH, D), 1.0),
        'positions': jnp.broadcast_to(jnp.arange(SEQ, dtype=jnp.int32)[None, :], (BATCH, SEQ)),
        'ada_w': nrm((DEPTH, D, 6 * D), 0.5 * D ** -0.5),
        'ada_b': nrm((DEPTH, 6 * D), 0.1),
        'norm1_g': 1.0 + nrm((DEPTH, D), 0.1),
        'norm2_g': 1.0 + nrm((DEPTH, D), 0.1),
        'ev_w_in': nrm((NE, D, EVEN_COLS), D ** -0.5),
        'ev_w_out': nrm((NE, 2 * MIX_HALF, D), (2 * MIX_HALF) ** -0.5),
        'nsa_pe_k': nrm((NE, CMP_BLOCK, HEAD_DIM), 0.1),
        'nsa_w1_k': nrm((NE, CMP_BLOCK * HEAD_DIM, CMP_HIDDEN), (CMP_BLOCK * HEAD_DIM) ** -0.5),
        'nsa_w2_k': nrm((NE, CMP_HIDDEN, HEAD_DIM), CMP_HIDDEN ** -0.5),
        'nsa_pe_v': nrm((NE, CMP_BLOCK, HEAD_DIM), 0.1),
        'nsa_w1_v': nrm((NE, CMP_BLOCK * HEAD_DIM, CMP_HIDDEN), (CMP_BLOCK * HEAD_DIM) ** -0.5),
        'nsa_w2_v': nrm((NE, CMP_HIDDEN, HEAD_DIM), CMP_HIDDEN ** -0.5),
        'gmlp_ln_g': 1.0 + nrm((NE, GMLP_GROUPS, MIX_HALF // GMLP_GROUPS), 0.1),
        'gmlp_ln_b': nrm((NE, GMLP_GROUPS, MIX_HALF // GMLP_GROUPS), 0.1),
        'gmlp_ws': nrm((NE, GMLP_GROUPS, GMLP_CHUNK, GMLP_CHUNK), GMLP_CHUNK ** -0.5),
        'gmlp_bs': 1.0 + nrm((NE, GMLP_GROUPS, GMLP_CHUNK), 0.1),
        'od_w_in': nrm((NO, D, ODD_COLS), D ** -0.5),
        'od_w_out': nrm((NO, 2 * MIX_HALF, D), (2 * MIX_HALF) ** -0.5),
        'rwkv_mu': jax.random.uniform(next(ks), (NO, RWKV_COLS), jnp.float32),
        'rwkv_w0': nrm((NO, MIX_HALF), 0.5),
        'rwkv_wB': nrm((NO, DECAY_LORA, MIX_HALF), DECAY_LORA ** -0.5),
        'rwkv_a0': nrm((NO, MIX_HALF), 0.5),
        'rwkv_aB': nrm((NO, ICLR_LORA, MIX_HALF), ICLR_LORA ** -0.5),
        'rwkv_gB': nrm((NO, GATE_LORA, MIX_HALF), GATE_LORA ** -0.5),
        'rwkv_xi': 0.85 + nrm((NO, MIX_HALF), 0.1),
        'rwkv_alpha': 1.0 + nrm((NO, MIX_HALF), 0.1),
        'rwkv_rho': nrm((NO, MIX_HALF), 0.1),
        'rwkv_ln_g': 1.0 + nrm((NO, RWKV_HEADS, HEAD_DIM), 0.1),
        'rwkv_ln_b': nrm((NO, RWKV_HEADS, HEAD_DIM), 0.1),
        'lru_conv_w': nrm((NO, LRU_CONV, LRU_WIDTH), 0.5),
        'lru_conv_b': nrm((NO, LRU_WIDTH), 0.1),
        'lru_wa': nrm((NO, LRU_BLOCKS, gw, gw), gw ** -0.5),
        'lru_ba': nrm((NO, LRU_WIDTH), 0.1),
        'lru_wx': nrm((NO, LRU_BLOCKS, gw, gw), gw ** -0.5),
        'lru_bx': nrm((NO, LRU_WIDTH), 0.1),
        'lru_lambda': lam,
        'ffn_up': nrm((DEPTH, D, F2), D ** -0.5),
        'ffn_conv_w': nrm((DEPTH, FFN_CONV, F2), FFN_CONV ** -0.5),
        'ffn_conv_b': nrm((DEPTH, F2), 0.1),
        'ffn_down': nrm((DEPTH, D_FF, D), D_FF ** -0.5),
        'final_g': 1.0 + nrm((D,), 0.1),
    }

def reference(x, c, positions, ada_w, ada_b, norm1_g, norm2_g, ev_w_in, ev_w_out,
              nsa_pe_k, nsa_w1_k, nsa_w2_k, nsa_pe_v, nsa_w1_v, nsa_w2_v,
              gmlp_ln_g, gmlp_ln_b, gmlp_ws, gmlp_bs, od_w_in, od_w_out,
              rwkv_mu, rwkv_w0, rwkv_wB, rwkv_a0, rwkv_aB, rwkv_gB, rwkv_xi, rwkv_alpha, rwkv_rho,
              rwkv_ln_g, rwkv_ln_b, lru_conv_w, lru_conv_b, lru_wa, lru_ba, lru_wx, lru_bx, lru_lambda,
              ffn_up, ffn_conv_w, ffn_conv_b, ffn_down, final_g):
    cos, sin = rope_tables(positions)
    cond = jax.nn.silu(c)
    for layer in range(DEPTH):
        i = layer // 2
        mod = cond @ ada_w[layer] + ada_b[layer]
        sh1, sc1, g1, sh2, sc2, g2 = jnp.split(mod, 6, axis=-1)
        h = modulate(rms_norm(x, norm1_g[layer]), sh1, sc1)
        if layer % 2 == 0:
            y = even_mixer(h, cos, sin, ev_w_in[i], ev_w_out[i], nsa_pe_k[i], nsa_w1_k[i], nsa_w2_k[i],
                           nsa_pe_v[i], nsa_w1_v[i], nsa_w2_v[i], gmlp_ln_g[i], gmlp_ln_b[i],
                           gmlp_ws[i], gmlp_bs[i])
        else:
            y = odd_mixer(h, od_w_in[i], od_w_out[i], rwkv_mu[i], rwkv_w0[i], rwkv_wB[i], rwkv_a0[i],
                          rwkv_aB[i], rwkv_gB[i], rwkv_xi[i], rwkv_alpha[i], rwkv_rho[i], rwkv_ln_g[i],
                          rwkv_ln_b[i], lru_conv_w[i], lru_conv_b[i], lru_wa[i], lru_ba[i], lru_wx[i],
                          lru_bx[i], lru_lambda[i])
        x = x + g1[:, None, :] * y
        h = modulate(rms_norm(x, norm2_g[layer]), sh2, sc2)
        x = x + g2[:, None, :] * conv_glu_ffn(h, ffn_up[layer], ffn_conv_w[layer], ffn_conv_b[layer], ffn_down[layer])
    return rms_norm(x, final_g)


_drawn_inputs = setup_inputs


def setup_inputs(seed=0):
    import zlib

    import numpy as np

    out = dict(_drawn_inputs(seed))
    spreads = {}
    factors = {'nsa_pe_k': 8.0,
     'nsa_w1_k': 3.532,
     'nsa_w2_k': 3.463,
     'nsa_pe_v': 7.523,
     'gmlp_ln_g': 4.513,
     'gmlp_ln_b': 4.283,
     'gmlp_bs': 3.313,
     'rwkv_wB': 2.95,
     'rwkv_xi': 8.0,
     'rwkv_alpha': 3.257,
     'rwkv_ln_g': 4.295,
     'rwkv_ln_b': 4.256,
     'lru_ba': 8.0,
     'lru_bx': 5.865}
    for name, (base, spread) in spreads.items():
        noise = np.random.default_rng([zlib.crc32(name.encode()), seed]).standard_normal(out[name].shape)
        drawn = base * np.exp(spread * noise) if base else spread * noise
        out[name] = __import__('jax').numpy.asarray(drawn.astype(out[name].dtype))
    for name, factor in factors.items():
        out[name] = (out[name] * factor).astype(out[name].dtype)
    return out
```

```python
import math
from contextlib import ExitStack

import numpy as np

import concourse.bass as bass
from concourse import mybir

F32, F16, BF16, I32 = mybir.dt.float32, mybir.dt.float16, mybir.dt.bfloat16, mybir.dt.int32
ALU = mybir.AluOpType
ACT = mybir.ActivationFunctionType
X = mybir.AxisListType.X

P = 128
T = 512
NT = T // P
D = 1024
KC = D // P
HD = 64
NH = 8
EPS = 1e-6
NEG = -1e30
NCMP = 31
FF = 2816
NF = FF // P
CONV = 3
ROPE = 16
THETA = 500000.0
WS = 64.0
HS = 4.0
INV = 1.0 / (WS * HS)
UNIT = 2048
U_KC, U_KS, U_Q, U_V, U_W1, U_GV, U_GU, U_OUT0, U_UP0, U_DOWN0 = 0, 1, 2, 4, 5, 9, 11, 13, 17, 39
U_IN1, U_OUT1, U_UP1, U_DOWN1, UNITS = 50, 61, 65, 87, 98
NV = 12
MAGIC = 12582912.0
G_NORM, G_STD, G_MIX = {2: 1, 5: 2, 8: 3, 12: 4, 14: 5, 17: 6}, 9, 23
G_SPLIT = 34
FIN_AT = {2: 4, 11: 5, 39: 6}

COLS = {}
_at = 0
for _name, _n in (
    ("c", 8), ("ada_b", 96), ("n1g0", 8), ("n2g0", 8), ("n1g1", 8), ("n2g1", 8), ("fg", 8),
    ("cw0", 3 * 2 * NF), ("cb0", 2 * NF), ("cw1", 3 * 2 * NF), ("cb1", 2 * NF),
    ("mu", 14), ("w0", 4), ("a0", 4), ("xi", 4), ("alpha", 4), ("rho", 4), ("lng", 4), ("lnb", 4),
    ("lcw", 16), ("lcb", 4), ("ba", 4), ("bx", 4), ("lam", 4), ("pek", 16), ("pev", 16), ("invf", 1),
):
    COLS[_name] = (_at, _n)
    _at += _n
NCOL = _at

MATS = {}
_at = 0
for _name, _n in (
    ("ident", 128), ("swap", 128), ("causal", 128), ("upper", 128), ("cmpadd", 128), ("cmpok", 128),
    ("wg", 192), ("w2k", 128), ("w2v", 128), ("ws", 1024), ("bs", 512), ("gln", 1024),
    ("head", 128), ("headcol", 2), ("sel8", 512),
    ("wab", 512), ("gb", 512), ("lwa", 512), ("lwx", 512),
):
    MATS[_name] = (_at, _n)
    _at += _n
NMAT = _at
MAT_EVEN = MATS["head"][0]
MAT_SEL = MATS["sel8"][0]
MAT_LORA = MATS["wab"][0]
MASKS = {"m0": 0, "m0t": 1, "strict": 2, "incl": 3, "level": 4}


def query_tile(g):
    return NT - 1 - g // 16


class Marks:

    def __init__(self, sem, names):
        self.sem, self.at, self.done = sem, {n: i + 1 for i, n in enumerate(names)}, 0
        assert len(self.at) == len(names)

    def hit(self, ins, name):
        self.done += 1
        assert self.at[name] == self.done, (name, self.done)
        ins.then_inc(self.sem, 1)

    def wait(self, eng, name):
        eng.wait_ge(self.sem, self.at[name])


class Own:

    def __init__(self, eng, sem):
        self.eng, self.sem, self.n = eng, sem, 0

    def __call__(self, ins):
        self.n += 1
        ins.then_inc(self.sem, 1)

    def wait(self):
        self.eng.wait_ge(self.sem, self.n)


def program(nc, wstream, ada, pcol, pmat, pmask, pos, xT, out):
    ctx = ExitStack()

    def sb(name, shape, dt=F32, stack=ctx):
        return stack.enter_context(nc.sbuf_tensor(name, shape, dt))

    def sem(name):
        return ctx.enter_context(nc.semaphore(name))

    x = sb("x", [P, KC, T])
    hh = sb("hh", [P, KC, T], F16)
    hl = sb("hl", [P, KC, T], F16)
    wraw = sb("wraw", [P, 2, UNIT])
    whi = sb("whi", [P, 2, UNIT], F16)
    wlo = sb("wlo", [P, 2, UNIT], F16)
    col = sb("col", [P, NCOL])
    mod = sb("mod", [P, 8 * NV])
    cond = sb("cond", [P, 8])
    gs4 = sb("gs4", [P, 8])
    sh4 = sb("sh4", [P, 8])
    cws = sb("cws", [P, 3 * 2 * NF])
    gres = sb("gres", [P, 8])
    sq = sb("sq", [P, 2, T])
    tn = sb("tn", [P, 2, T])
    h4 = sb("h4", [P, 2, T])
    ss = sb("ss", [P, 4])
    rs = sb("rs", [P, 4])
    dg = sb("dg", [P, 4, P])
    rstd = sb("rstd", [P, T])
    ones = sb("ones", [P, P])
    ident = sb("ident", [P, P])
    PS = ctx.enter_context(nc.psum_tensor("PS", [P, 8, 512], F32))

    def pc(name, a=0, n=None):
        at, size = COLS[name]
        return col[:, at + a:at + (size if n is None else a + n)]

    def pm(name, a=0, n=None):
        at, size = MATS[name]
        return mat[:, at + a:at + (size if n is None else a + n)]

    adas = ExitStack()
    adab = sb("adab", [P, 4, D], stack=adas)
    adacc = sb("adacc", [P, 2, D], stack=adas)
    adprod = sb("adprod", [P, D], stack=adas)

    even = ExitStack()

    def se(name, shape, dt=F32):
        return sb(name, shape, dt, even)

    mat = se("mat", [P, MAT_EVEN])
    cosT = se("cosT", [P, T])
    sinT = se("sinT", [P, T])
    posi = se("posi", [P, T], I32)
    kco = se("kco", [P, 4 * (T + 1)])
    kcS = kco[:].rearrange("p (c h t) -> p c h t", c=2, h=2)
    oacc = kco[:, 0:NT * T].rearrange("p (m n) -> p m n", m=NT)
    kcG = se("kcG", [P, 16, 2, NCMP])
    gch = se("gch", [P, 2, 16, 2, NCMP], F16)
    gcl = se("gcl", [P, 2, 16, 2, NCMP], F16)
    hidc = se("hidc", [P, 2, 2, 2, 32])
    kcr = se("kcr", [P, 32])
    kct = se("kct", [P, 2, 32])
    kcmp = se("kcmp", [P, 32])
    vcmp = se("vcmp", [P, 4, HD])
    work = se("work", [P, 6, T])
    xr, rt = work[:, 0:4], work[:, 4:6]
    Pb, PTs = work[:, 0:3], work[:, 3:5]
    ot = work[:, 5].rearrange("p (h d) -> p h d", d=HD)
    q = se("q", [P, 4, T])
    ksw = se("ksw", [P, 2, T])
    vsw = se("vsw", [P, NT, 256])
    wgh = se("wgh", [P, 8, 24], F16)
    wgl = se("wgl", [P, 8, 24], F16)
    gates = se("gates", [P, NT, 24])
    gu = se("gu", [P, 4, T])
    gv = se("gv", [P, NT, T])
    gsq = (sq, tn)
    yt = h4

    def xn(j):
        return gv[:, j] if j < 4 else gu[:, j - 4]

    gm = se("gm", [P, 32])
    gr = se("gr", [P, 32])
    identb = se("identb", [P, P], BF16)
    causb = se("causb", [P, P], BF16)
    nmax = se("nmax", [P, 64])
    sums = se("sums", [P, 64])
    rc = se("rc", [P, 8])
    sc = se("sc", [P, 8])
    cs = se("cs", [P, 8, 32])
    cp = se("cp", [P, 2, 8, 32])
    cm = se("cm", [P, 8])
    csum = se("csum", [P, 4, 8])
    ptc = se("ptc", [P, 2, P])
    even.close()

    glu = ExitStack()
    hidh = sb("hidh", [P, NF, T], F16, glu)
    hidl = sb("hidl", [P, NF, T], F16, glu)
    cv = sb("cv", [P, 2, 2, T], stack=glu)
    sa = sb("sa", [P, 2, T], stack=glu)
    prod = sb("prod", [P, 2, T], stack=glu)
    glu.close()
    adas.close()

    odd = ExitStack()

    def so(name, shape, dt=F32):
        return sb(name, shape, dt, odd)

    r_, k_, v_, epp, ep, em, kap, al, og = (so(n, [P, 4, T]) for n in ("r_", "k_", "v_", "epp", "ep", "em", "kap", "al", "og"))
    big = so("big", [P, 6, 4, T])
    rr, ii, aa, gl, xc, sqk = (big[:, n] for n in range(6))
    Zt = big[:, 0:2].rearrange("p a j t -> p (a j) t")
    RBt = big[:, 2:4].rearrange("p a j t -> p (a j) t")
    W1 = big[:, 4]
    Yl = big[:, 5]
    AT, Xm, Y1 = sq, tn, h4
    lmat = v_[:].rearrange("p j t -> p (j t)")
    lt = em[:, 0:2]
    bT, kT, VT = em, ep, v_
    KM = hl[:, 0:4].rearrange("p j t -> p (j t)").bitcast(F32).rearrange("p (h t) -> p h t", h=2)
    UG = hh[:, 0:4].rearrange("p j t -> p (j t)").bitcast(F32).rearrange("p (h t) -> p h t", h=2)
    rkT = h4[0:8, 0]
    Sst = kap[:, 0].rearrange("p (s n) -> p s n", s=2)
    resetm = dg[:].rearrange("p m t -> p (m t)")
    sel8 = rstd[0:8, :]
    mo = so("mo", [P, MAT_SEL - MAT_EVEN])
    mk = so("mk", [P, 10, P], F16)
    small, at = {}, 0
    for name, n in (("spl", 12), ("mus", 28), ("lcs", 16), ("oal", 4), ("ec", 16), ("rmid", 16), ("rk", 32)):
        small[name] = cws[:, at:at + n]
        at += n
    assert at <= 3 * 2 * NF
    spl = small["spl"].rearrange("p (s j) -> p s j", s=3)
    mus = small["mus"].rearrange("p (s j) -> p s j", s=2)
    lcs, oal, rk = small["lcs"], small["oal"], small["rk"]
    ec = small["ec"].rearrange("p (j c) -> p j c", j=4)
    rmid = small["rmid"].rearrange("p (j c) -> p j c", j=4)
    odd.close()

    def po(name, a=0, n=None):
        at, size = MATS[name]
        at -= MAT_EVEN
        return mo[:, at + a:at + (size if n is None else a + n)]

    def mask(name, a=0):
        return mk[:, MASKS[name] + a].unsqueeze(1).to_broadcast([P, 4, P])

    w_ready = [sem("w_ready0"), sem("w_ready1")]
    w_hi, w_lo, unit_done = sem("w_hi"), sem("w_lo"), sem("unit_done")
    cols_in, mats_in, x_in, pos_in, out_done = (sem(n) for n in ("cols_in", "mats_in", "x_in", "pos_in", "out_done"))
    ada_ready = [sem(f"ada_ready{i}") for i in range(4)]
    ada_more = [sem(f"ada_more{i}") for i in range(4)]
    ada_read, ada_done, fin_pe, fin_dve = (sem(n) for n in ("ada_read", "ada_done", "fin_pe", "fin_dve"))
    pool_own, act_own, dve_own = sem("pool_own"), sem("act_own"), sem("dve_own")
    const_ready, cond_ready = sem("const_ready"), sem("cond_ready")
    sq_ready, ss_dve, ss_act, dg_ready, rb_pe, rstd_ready, tn_ready, h_hi, h_lo, x_upd = (
        sem(n) for n in ("sq_ready", "ss_dve", "ss_act", "dg_ready", "rb_pe", "rstd_ready", "tn_ready",
                         "h_hi", "h_lo", "x_upd"))
    sq_used, gs_ready = sem("sq_used"), sem("gs_ready")
    rope_arg, rope_tab = sem("rope_arg"), sem("rope_tab")
    kc_shift, xr_ready, swap_done, rope_done = (sem(n) for n in ("kc_shift", "xr_ready", "swap_done", "rope_done"))
    g_built, g_hi, g_lo, v_evac, gate_pe, hid_ready, cmp_pe, cmp_act, cmp_swap, cmp_dve = (
        sem(n) for n in ("g_built", "g_hi", "g_lo", "v_evac", "gate_pe", "hid_ready", "cmp_pe", "cmp_act", "cmp_swap", "cmp_dve"))
    wg_hi, gv_ready, gvar_ready, gstd_ready, gn_ready, gu_ready, gmix_pe, gmix_t, y_hi, y_lo = (
        sem(n) for n in ("wg_hi", "gv_ready", "gvar_ready", "gstd_ready", "gn_ready", "gu_ready", "gmix_pe", "gmix_t", "y_hi", "y_lo"))
    c_S, c_sub, c_exp, c_P, c_T, c_ev, c_V, c_O = (sem(n) for n in ("c_S", "c_sub", "c_exp", "c_P", "c_T", "c_ev", "c_V", "c_O"))
    a_S, a_max, a_exp, a_T, a_evA, a_evD, a_V, a_O, o_T = (
        sem(n) for n in ("a_S", "a_max", "a_exp", "a_T", "a_evA", "a_evD", "a_V", "a_O", "o_T"))

    cws_ready, tap_in, tap1, tap_done, silu_done, prod_done, hid_hi, hid_lo, down_done = (
        sem(n) for n in ("cws_ready", "tap_in", "tap1", "tap_done", "silu_done", "prod_done", "hid_hi", "hid_lo",
                         "down_done"))

    ident_in, mo_in = sem("ident_in"), sem("mo_in")
    pairs = range(4)
    OP = Marks(sem("odd_pe"), ["lru_r", "lru_i", "pre_w", "pre_a", "pre_g", "kk", "rkT"]
               + [("ksp", j) for j in pairs]
               + [n for j in pairs for n in
                  [("bon", j), ("A", j), ("AT", j), ("KM", j)]
                  + [m for l in range(1, 7) for m in
                     [("Y", j, l, 0), ("Y", j, l, 1)] + [[("RB", j)], [("RK", j)], [("TV", j)], [("TB", j), ("TK", j)], [("W", j)], [("YL", j)]][l - 1]
                     + [("XZ", j, l, 0), ("XZ", j, l, 1)]]]
               + [n for c in range(4) for n in [("G", c), ("U", c)] + ([("S", c)] if c < 3 else []) + [("Yc", c)]]
               + [("mean", j) for j in pairs] + ["var", "vT"] + [("vsp", j) for j in pairs])
    OD = Marks(sem("odd_dve"), ["shift_par", "lru_b", "kap", "yd", "cum", "ec", "dd", "rkv", "rki", "rkTc"] + [("ksp", j) for j in pairs] + [("brk", 0), ("prep", 0)]
               + [n for j in pairs for n in
                  [("bon", j), ("X0", j), ("Z0", j), ("KM", j)]
                  + [m for l in range(1, 7) for m in
                     [("Y", j, l, 0), ("Y", j, l, 1)] + ([("RB", j)] if l == 1 else [("RK", j)] if l == 2 else [])
                     + [("XZ", j, l, 0), ("XZ", j, l, 1)]
                     + ([("brk", j + 1), ("prep", j + 1)] if l == 4 and j < 3 else [])]]
               + ["S0"] + [n for c in range(4) for n in [("G", c)] + ([("S", c)] if c < 3 else []) + [("Yc", c)]]
               + [("cen", j) for j in pairs] + ["rkv2", "rki2", "rkT2"] + [("y", j) for j in pairs])
    OA = Marks(sem("odd_act"), ["lru_r", "lru_i", "lru_e", "lru_t", "lora", "lw", "lru_s", "av", "g"]
               + ["exp_m", "exp_p", "exp_pp", "exp_c", "rks", "ydh"]
               + [n for j in pairs for n in [("AT", j), ("VT", j), ("bT", j), ("kT", j), ("W", j), ("YL", j)]]
               + [("U", c) for c in range(4)] + [("sq", j) for j in pairs] + ["rks2"] + [("y", j) for j in pairs])
    o_in, o_sh, spl_ready, ydl_ready = (sem(n) for n in ("o_in", "o_sh", "spl_ready", "ydl_ready"))
    KSP = (4, 5, 6, 7)

    def ss_bank(n):
        return 0 if n in (2, 4) else 4

    def fin_bank(v):
        return 6 if v in (1, 9, 11) else 7

    block = ctx.enter_context(nc.Block())

    @block.sync
    def _(sp):
        sp.dma_start(col[:], pcol).then_inc(cols_in, 16)
        sp.dma_start(posi[:], pos).then_inc(pos_in, 16)

        def load_ada(n):
            if n >= 4:
                sp.wait_ge(ada_read, n - 3)
            sp.dma_start(adab[:, n % 4], ada[n]).then_inc(ada_ready[n % 4], 16)

        for n in range(16):
            load_ada(n)
            if n == 3:
                sp.dma_start(mat[:, 0:P], pmat[:, 0:P]).then_inc(ident_in, 16)
            if n == 10:
                sp.dma_start(wraw[:, 0], wstream[0]).then_inc(w_ready[0], 16)
        sp.dma_start(wraw[:, 1], wstream[1]).then_inc(w_ready[1], 16)
        sp.dma_start(mat[:, P:MAT_EVEN], pmat[:, P:MAT_EVEN]).then_inc(mats_in, 16)
        with sp.Fori(1, UNITS // 2) as i:
            for s in range(2):
                sp.wait_ge(w_lo, 2 * i + s - 1)
                sp.dma_start(wraw[:, s], wstream[bass.ds(2 * i + s, 1)].rearrange("o p n -> p (o n)")).then_inc(w_ready[s], 16)
        sp.wait_ge(out_done, 16 * 8)

    @block.gpsimd
    def _(pool):
        def load(n):
            pool.dma_start(adab[:, (n % 4) if isinstance(n, int) else n[1]],
                           ada[n] if isinstance(n, int) else ada[bass.ds(n[0], 1)].rearrange("o p n -> p (o n)"))\
                .then_inc(ada_more[(n % 4) if isinstance(n, int) else n[1]], 16)

        pool.wait_ge(x_in, 32)
        pool.wait_ge(rstd_ready, 1)
        for j in range(8):
            pool.tensor_tensor(xn(j), x[:, j], rstd[:], ALU.mult).then_inc(tn_ready, 1)

        for n in range(16, 20):
            pool.wait_ge(ada_read, n - 3)
            load(n)

        def pair(i, last):
            for s in range(2):
                pool.wait_ge(fin_pe, 2 * i + s + 1)
                for k in range(8):
                    m = 8 * s + k
                    pool.wait_ge(ada_more[k % 4], 16 * (4 * i + (m // 4) + 1))
                    dst = adacc[:, s] if k == 0 else adprod[:]
                    pool.tensor_tensor(dst, adab[:, k % 4], cond[:, k:k + 1].to_broadcast([P, D]), ALU.mult).then_inc(pool_own, 1)
                    step = 15 * s + (1 if k == 0 else 2 * k)
                    pool.wait_ge(pool_own, 30 * i + step)
                    if not (last and m >= 12):
                        load((16 + 16 * i + m + 4, k % 4))
                    if k:
                        pool.tensor_tensor(adacc[:, s], adacc[:, s], adprod[:], ALU.add).then_inc(pool_own, 1)
                        pool.wait_ge(pool_own, 30 * i + step + 1)
                pool.sem_inc(ada_done, 1)

        with pool.Fori(0, 4) as i:
            pair(i, False)
        pair(4, True)
        OA.wait(pool, "ydh")
        pool.tensor_tensor(hl[:, 4:8], xc, hh[:, 4:8], ALU.subtract).then_inc(ydl_ready, 1)

    @block.scalar
    def _(act):
        own = Own(act, act_own)

        def split_hi(u, quarter=None):
            if isinstance(u, int) and u >= UNITS:
                return
            s, turn = (u % 2, u // 2) if isinstance(u, int) else u
            act.wait_ge(w_ready[s], 16 * (turn + 1))
            n = slice(0, UNIT) if quarter is None else slice(UNIT // 4 * quarter, UNIT // 4 * (quarter + 1))
            ins = act.activation(whi[:, s, n], wraw[:, s, n], ACT.Copy, scale=WS)
            if n.stop == UNIT:
                ins.then_inc(w_hi, 1)

        def square(n, j):
            if n == 0:
                act.wait_ge(x_in, 32)
            else:
                act.wait_ge(x_upd, 8 * (n - 1) + j + 1)
            if 8 * n + j >= 2:
                act.wait_ge(sq_used, 8 * n + j - 1)
            act.activation(sq[:, j % 2], x[:, j], ACT.Square).then_inc(sq_ready, 1)

        def norm_root(n):
            act.wait_ge(ss_dve, n + 1)
            act.activation(ss[:], ss[:], ACT.Sqrt).then_inc(ss_act, 1)

        def norm_apply(n):
            if n == 0:
                act.wait_ge(gs_ready, 1)
            for j in range(8):
                act.wait_ge(tn_ready, 8 * n + j + 1)
                if 8 * n + j >= 2:
                    act.wait_ge(h_lo, 8 * n + j - 1)
                src = tn[:, j % 2] if n else xn(j)
                act.activation(h4[:, j % 2], src, ACT.Identity, scale=gs4[:, j:j + 1], bias=sh4[:, j:j + 1])
                act.activation(hh[:, j], src, ACT.Identity, scale=gs4[:, j:j + 1], bias=sh4[:, j:j + 1])\
                    .then_inc(h_hi, 1)

        def out_phase(n, base):
            for i in range(4):
                act.wait_ge(unit_done, base + i + 1)
                split_hi(base + i + 2)
                square(n, 2 * i)
                square(n, 2 * i + 1)
            norm_root(n)
            norm_apply(n)

        def glu_up(l, base):
            act.wait_ge(cws_ready, l + 1)
            cb = COLS[f"cb{l}"][0]
            with act.Fori(0, NF // 2) as i:
                for s in range(2):
                    j = 2 * i + s
                    b = (base + s) % 2
                    act.wait_ge(unit_done, base + 1 + j)
                    for c in range(2):
                        act.activation(cv[:, s, c], PS[:, 2 * b + c, :], ACT.Identity,
                                       scale=cws[:, bass.ds(4 * NF + c * NF + j, 1)], bias=col[:, bass.ds(cb + c * NF + j, 1)])\
                            .then_inc(tap_in, 1)
                    split_hi((b, i + (base + s + 2) // 2))
                    act.wait_ge(tap_done, 2 * NF * l + 1 + 2 * j)
                    act.activation(sa[:, s], cv[:, s, 0], ACT.Silu).then_inc(silu_done, 1)
                    act.wait_ge(prod_done, NF * l + 1 + j)
                    act.activation(hidh[:, bass.ds(j, 1), :].rearrange("p o t -> p (o t)"), prod[:, s], ACT.Copy).then_inc(hid_hi, 1)

        def odd_mats():
            act.wait_ge(fin_pe, NV)
            act.wait_ge(x_upd, 16)
            act.dma_start(mo[:], pmat[:, MAT_EVEN:MAT_SEL]).then_inc(mo_in, 16)
            act.dma_start(mk[:].rearrange("p n t -> p (n t)"), pmask).then_inc(mo_in, 16)
            act.dma_start(lmat, pmat[:, MAT_LORA:NMAT]).then_inc(mo_in, 16)

        def glu_down(n, base):
            with act.Fori(0, 4) as i:
                for s in range(2):
                    act.wait_ge(unit_done, base + 1 + 2 * i + s)
                    split_hi(((base + s) % 2, i + (base + s + 2) // 2))
            for u in (base + 8, base + 9):
                act.wait_ge(unit_done, u + 1)
                split_hi(u + 2)
            for j in range(8):
                square(n, j)
            act.wait_ge(unit_done, base + 11)
            split_hi(base + 12)
            norm_root(n)
            if n == 2:
                odd_mats()
            if n < 4:
                norm_apply(n)

        act.dma_start(x[:, 0:4], xT[:, 0:4]).then_inc(x_in, 16)
        act.dma_start(x[:, 4:8], xT[:, 4:8]).then_inc(x_in, 16)
        act.wait_ge(cols_in, 16)
        act.activation(cond[:], pc("c"), ACT.Silu).then_inc(cond_ready, 1)
        for j in range(8):
            square(0, j)
        norm_root(0)
        split_hi(0)
        split_hi(1)
        norm_apply(0)
        act.wait_ge(mats_in, 16)
        act.activation(wgh[:].rearrange("p k n -> p (k n)"), pm("wg"), ACT.Copy, scale=WS).then_inc(wg_hi, 1)
        for n, tab in enumerate((sinT, cosT)):
            act.wait_ge(rope_arg, n + 1)
            act.activation(tab[:], xr[:, n], ACT.Sin).then_inc(rope_tab, 1)

        act.wait_ge(unit_done, 1)
        for c in range(2):
            own(act.activation(kcS[0:64, c, 0, 1:T + 1], PS[0:64, c, :], ACT.Copy, scale=INV))
            own(act.activation(kcS[64:128, c, 1, 0:T], PS[64:128, c, :], ACT.Copy, scale=INV))
        split_hi(2)
        own.wait()
        act.dma_start(kcS[64:128, :, 0, 0:T], kcS[0:64, :, 0, 1:T + 1]).then_inc(kc_shift, 16)
        act.dma_start(kcS[0:64, :, 1, 1:T + 1], kcS[64:128, :, 1, 0:T]).then_inc(kc_shift, 16)
        for u in (1, 2, 3):
            act.wait_ge(unit_done, u + 1)
            for c in range(2):
                r = 2 * (u - 1) + c
                if r >= 4:
                    act.wait_ge(rope_done, r - 3)
                act.activation(xr[:, r % 4], PS[:, 2 * (u % 2) + c, :], ACT.Copy,
                               scale=INV if u == 1 else INV * HD ** -0.5).then_inc(xr_ready, 1)
            split_hi(u + 2)
        act.wait_ge(g_built, 1)
        act.activation(gch[:, 0].rearrange("p l h n -> p (l h n)"), kcG[:].rearrange("p l h n -> p (l h n)"), ACT.Copy)\
            .then_inc(g_hi, 1)
        act.wait_ge(unit_done, U_V + 1)
        for c in range(2):
            act.activation(vsw[:, 2 * c:2 * c + 2].rearrange("p m n -> p (m n)"), PS[:, c, :], ACT.Copy, scale=INV).then_inc(v_evac, 1)
        split_hi(U_V + 2)
        act.wait_ge(g_built, 2)
        act.activation(gch[:, 1].rearrange("p l h n -> p (l h n)"), kcG[:].rearrange("p l h n -> p (l h n)"), ACT.Copy)\
            .then_inc(g_hi, 1)
        act.wait_ge(gate_pe, 1)
        act.activation(gates[:].rearrange("p m n -> p (m n)"), PS[:, 6, 0:96], ACT.Sigmoid, scale=INV).then_inc(v_evac, 1)
        for c in range(2):
            u = U_W1 + 2 * c
            act.wait_ge(unit_done, u + 1)
            split_hi(u + 2)
            act.wait_ge(unit_done, u + 2)
            for ct in range(2):
                act.activation(hidc[:, c, ct, :, 0:NCMP], PS[:, 2 + 2 * c + ct, 0:62].rearrange("p (h n) -> p h n", h=2),
                               ACT.Gelu_apprx_tanh, scale=1.0 / WS).then_inc(hid_ready, 1)
            split_hi(u + 3)

        def c_exps(i):
            act.wait_ge(c_sub, i + 1)
            act.activation(cp[:, i % 2], cs[:], ACT.Exp).then_inc(c_exp, 1)

        def exps(g):
            i = query_tile(g)
            act.wait_ge(a_max, g + 1)
            if g >= 3:
                act.wait_ge(a_T, g - 2)
            act.activation(Pb[:, g % 3, 0:(i + 1) * P], PS[:, (g + 2) % 3, 0:(i + 1) * P], ACT.Exp, bias=nmax[:, g:g + 1],
                           accum_out=sums[:, g:g + 1]).then_inc(a_exp, 1)

        for u in (U_GV, U_GV + 1, U_GU, U_GU + 1):
            act.wait_ge(unit_done, u + 1)
            for b in range(2):
                if u < U_GU:
                    c = u - U_GV
                    act.activation(gv[:, 2 * b:2 * b + 2, 256 * c:256 * c + 256],
                                   PS[:, 2 * (u % 2) + b, :].rearrange("p (m n) -> p m n", m=2),
                                   ACT.Gelu_apprx_tanh, scale=INV).then_inc(gv_ready, 1)
                else:
                    act.activation(gu[:, 2 * (u - U_GU) + b], PS[:, 2 * (u % 2) + b, :], ACT.Gelu_apprx_tanh, scale=INV).then_inc(gu_ready, 1)
            if u == U_GV + 1:
                c_exps(1)
            if u == U_GU:
                c_exps(3)
            if u < U_GU:
                split_hi(u + 2)
            if u == U_GU:
                exps(0)
            if u == U_GV:
                act.wait_ge(cmp_pe, 1)
                act.activation(kcr[:], PS[:, 4, 0:32], ACT.Copy).then_inc(cmp_act, 1)
                act.wait_ge(const_ready, 15)
                for s4 in range(4):
                    act.activation(vcmp[32 * s4:32 * s4 + 32, s4, :], PS[32 * s4:32 * s4 + 32, 6, 0:HD], ACT.Copy).then_inc(cmp_act, 1)
                c_exps(0)
            if u == U_GV + 1:
                c_exps(2)

        def g_hi_part(j):
            act.wait_ge(gmix_t, j + 1)
            act.activation(hh[:, 4 + j], yt[:, j % 2], ACT.Copy).then_inc(y_hi, 1)

        def o_hi(n):
            i = NT - 1 - n
            act.wait_ge(o_T, n + 1)
            act.activation(hh[:, 0:4, i * P:(i + 1) * P], PS[:, 7, :].rearrange("p (f t) -> p f t", f=4), ACT.Copy).then_inc(y_hi, 1)

        for g in range(64):
            i = query_tile(g)
            if g + 1 < 64:
                exps(g + 1)
            if 0 <= g - G_SPLIT < 8:
                split_hi(U_OUT0 + (g - G_SPLIT) // 4, (g - G_SPLIT) % 4)
            if g % 2 == 0:
                act.wait_ge(a_T, g + 1)
                if g >= 2:
                    act.wait_ge(a_V, g - 1)
                act.activation(PTs[:, 0, 0:(i + 1) * P], PS[:, 3, 0:(i + 1) * P], ACT.Copy).then_inc(a_evA, 1)
            if g == G_STD:
                act.wait_ge(gvar_ready, 1)
                act.activation(gm[:], gr[:], ACT.Sqrt).then_inc(gstd_ready, 1)
            if g % 16 == 6 and g > 16:
                o_hi(g // 16 - 1)
            for j in range(4):
                if g == G_MIX + 3 * j + 2:
                    g_hi_part(j)
        o_hi(3)
        out_phase(1, U_OUT0)
        glu_up(0, U_UP0)
        glu_down(2, U_DOWN0)

        act.dma_start(sel8, pmat[0:8, MAT_SEL:MAT_LORA]).then_inc(mo_in, 16)
        own(act.activation(spl[:, 0], pc("lam"), ACT.Abs))
        own.wait()
        own(act.activation(spl[:, 0], spl[:, 0], ACT.Exp, scale=-1.0))
        own.wait()
        act.activation(spl[:, 0], spl[:, 0], ACT.Ln, bias=1.0).then_inc(spl_ready, 1)
        OD.wait(act, "shift_par")
        for i in range(2):
            act.wait_ge(unit_done, U_IN1 + i + 1)
            for c in range(2):
                j = 2 * i + c
                act.activation(xc[:, j], PS[:, 2 * (i % 2) + c, :], ACT.Identity, scale=lcs[:, 12 + j:13 + j], bias=pc("lcb", j, 1))\
                    .then_inc(o_in, 1)
            split_hi(U_IN1 + i + 2)
        def sigmoid4(dst, bias, name):
            OP.wait(act, name)
            for j in range(4):
                ins = act.activation(dst[:, j], PS[:, 4 + j, :], ACT.Sigmoid, bias=pc(bias, j, 1))
            return ins

        for i in (2, 3):
            act.wait_ge(unit_done, U_IN1 + i + 1)
            for c in range(2):
                act.activation(gl[:, 2 * (i - 2) + c], PS[:, 2 * (i % 2) + c, :], ACT.Gelu_apprx_tanh, scale=INV)
            split_hi(U_IN1 + i + 2)
            if i == 2:
                OA.hit(sigmoid4(rr, "ba", "lru_r"), "lru_r")

        def shifted(i, dst, m):
            act.wait_ge(unit_done, U_IN1 + i + 1)
            for c in range(2):
                act.activation(dst[:, c], PS[:, 2 * (i % 2) + c, :], ACT.Identity, scale=mus[:, 1, m + c:m + c + 1]).then_inc(o_in, 1)
            split_hi(U_IN1 + i + 2)

        shifted(4, lt, 12)
        OA.hit(sigmoid4(ii, "bx", "lru_i"), "lru_i")
        act.wait_ge(o_sh, 14)
        OA.wait(act, "lru_r")
        for j in range(4):
            ins = act.activation(aa[:, j], rr[:, j], ACT.Exp, scale=spl[:, 1, j:j + 1])
        OA.hit(ins, "lru_e")
        for j in range(4):
            ins = act.activation(rr[:, j], rr[:, j], ACT.Tanh, scale=spl[:, 2, j:j + 1])
        OA.hit(ins, "lru_t")
        shifted(5, k_[:, 0:2], 4)
        own(act.activation(lt[0:64, 0], lt[0:64, 0], ACT.Tanh))
        OA.hit(act.activation(lt[:, 1], lt[:, 1], ACT.Sigmoid), "lora")
        shifted(6, k_[:, 2:4], 6)
        OA.hit(sigmoid4(epp, "w0", "pre_w"), "lw")
        OD.wait(act, "lru_b")
        OA.hit(act.activation(rr, rr, ACT.Sqrt), "lru_s")
        shifted(7, r_[:, 0:2], 0)
        OA.hit(sigmoid4(al, "a0", "pre_a"), "av")
        shifted(8, r_[:, 2:4], 2)
        OP.wait(act, "pre_g")
        for j in range(4):
            ins = act.activation(og[:, j], PS[:, 4 + j, :], ACT.Copy)
        OA.hit(ins, "g")
        OD.wait(act, "dd")
        OA.hit(act.activation(em[:], ep[:], ACT.Exp, scale=-1.0), "exp_m")
        OA.hit(act.activation(ep[:], ep[:], ACT.Exp), "exp_p")
        OA.hit(act.activation(epp[:], epp[:], ACT.Exp), "exp_pp")
        OA.hit(act.activation(ec[:], ec[:], ACT.Exp), "exp_c")
        OD.wait(act, "rkv")
        OA.hit(act.activation(rk[:], rk[:], ACT.Sqrt), "rks")
        shifted(9, v_[:, 0:2], 8)
        shifted(10, v_[:, 2:4], 10)
        OD.wait(act, "yd")
        OA.hit(act.activation(hh[:, 4:8], xc, ACT.Copy), "ydh")
        for j in pairs:
            OP.wait(act, ("AT", j))
            if j:
                OP.wait(act, ("XZ", j - 1, 6, 1))
            for h in range(2):
                ins = act.activation(AT[:, h], PS[:, 4 + h, :], ACT.Copy)
            OA.hit(ins, ("AT", j))
            OP.wait(act, ("TV", j))
            OA.hit(act.activation(VT[:, j], PS[:, 6, :], ACT.Copy), ("VT", j))
            OP.wait(act, ("TB", j))
            OA.hit(act.activation(bT[:, j], PS[:, 7, :], ACT.Copy), ("bT", j))
            OP.wait(act, ("TK", j))
            OA.hit(act.activation(kT[:, j], PS[:, 6, :], ACT.Copy), ("kT", j))
            OP.wait(act, ("W", j))
            if j == 0:
                act.wait_ge(ydl_ready, 1)
            for h in range(2):
                ins = act.activation(W1[:, :, 256 * h + HD * j:256 * h + HD * j + HD],
                                     PS[:, 7, :].rearrange("p (c h d) -> p c h d", c=4, h=2)[:, :, h], ACT.Copy)
            OA.hit(ins, ("W", j))
            OP.wait(act, ("YL", j))
            OA.hit(act.activation(Yl[:, j], PS[:, 6, :], ACT.Copy), ("YL", j))
        for c in range(4):
            OP.wait(act, ("U", c))
            OA.hit(act.activation(UG[:, 0], PS[:, 0, :], ACT.Copy), ("U", c))
        for j in pairs:
            OD.wait(act, ("cen", j))
            OA.hit(act.activation(em[:, j], Yl[:, j], ACT.Square), ("sq", j))
        OD.wait(act, "rkv2")
        OA.hit(act.activation(rk[:], rk[:], ACT.Sqrt), "rks2")
        for j in pairs:
            OD.wait(act, ("y", j))
            OA.hit(act.activation(hh[:, j], Yl[:, j], ACT.Copy), ("y", j))
        out_phase(3, U_OUT1)
        glu_up(1, U_UP1)
        glu_down(4, U_DOWN1)
        for j in range(8):
            dst = r_[:, j] if j < 4 else k_[:, j - 4]
            act.wait_ge(tn_ready, 33 + j)
            act.activation(dst, tn[:, j % 2], ACT.Identity, scale=pc("fg", j, 1)).then_inc(h_hi, 1)
            act.wait_ge(h_hi, 33 + j)
            act.dma_start(out[:, j], dst).then_inc(out_done, 16)

    @block.vector
    def _(dve):
        own = Own(dve, dve_own)

        def split_lo(u, quarter=None):
            if isinstance(u, int) and u >= UNITS:
                return
            s, turn = (u % 2, u // 2) if isinstance(u, int) else u
            dve.wait_ge(w_hi, 2 * turn + s + 1)
            n = slice(0, UNIT) if quarter is None else slice(UNIT // 4 * quarter, UNIT // 4 * (quarter + 1))
            ins = dve.scalar_tensor_tensor(wlo[:, s, n], wraw[:, s, n], WS, whi[:, s, n], ALU.mult, ALU.subtract)
            if n.stop == UNIT:
                ins.then_inc(w_lo, 1)

        def fin(v):
            dve.wait_ge(fin_pe, v + 1)
            dve.tensor_tensor(mod[:, 8 * v:8 * v + 8], PS[:, fin_bank(v), 0:8], pc("ada_b", 8 * v, 8), ALU.add).then_inc(fin_dve, 1)

        def out_phase(base, v):
            dve.wait_ge(fin_dve, v + 1)
            own(dve.tensor_scalar(gres[:], mod[:, 8 * v:8 * v + 8], 1.0 / WS, None, ALU.mult))
            own.wait()
            for i in range(4):
                dve.wait_ge(unit_done, base + i + 1)
                for c in range(2):
                    j = 2 * i + c
                    dve.scalar_tensor_tensor(x[:, j], PS[:, 2 * ((base + i) % 2) + c, :], gres[:, j:j + 1], x[:, j], ALU.mult, ALU.add)\
                        .then_inc(x_upd, 1)
                split_lo(base + i + 2)

        def glu_up(l, base):
            with dve.Fori(0, NF // 2) as i:
                for s in range(2):
                    j = 2 * i + s
                    b = (base + s) % 2
                    for tap in (1, 0):
                        for c in range(2):
                            if tap:
                                dve.wait_ge(tap_in, 2 * NF * l + 1 + 2 * j + c)
                            else:
                                dve.wait_ge(tap1, 2 * NF * l + 1 + 2 * j + c)
                            d = 2 - tap
                            dve.scalar_tensor_tensor(cv[:, s, c, d:T], PS[:, 2 * b + c, 0:T - d],
                                                     cws[:, bass.ds(2 * NF * tap + c * NF + j, 1)], cv[:, s, c, d:T], ALU.mult, ALU.add)\
                                .then_inc(tap1 if tap else tap_done, 1)
                    split_lo((b, i + (base + s + 2) // 2))
                    dve.wait_ge(silu_done, NF * l + 1 + j)
                    dve.wait_ge(tap_done, 2 * NF * l + 2 + 2 * j)
                    dve.tensor_tensor(prod[:, s], sa[:, s], cv[:, s, 1], ALU.mult).then_inc(prod_done, 1)
                    dve.wait_ge(hid_hi, NF * l + 1 + j)
                    dve.tensor_tensor(hidl[:, bass.ds(j, 1), :].rearrange("p o t -> p (o t)"), prod[:, s],
                                      hidh[:, bass.ds(j, 1), :].rearrange("p o t -> p (o t)"), ALU.subtract).then_inc(hid_lo, 1)

        def glu_down(l, base, v):
            dve.wait_ge(fin_dve, v + 1)
            own(dve.tensor_scalar(gres[:], mod[:, 8 * v:8 * v + 8], 1.0 / WS, None, ALU.mult))
            own.wait()
            with dve.Fori(0, 4) as i:
                for s in range(2):
                    dve.wait_ge(unit_done, base + 1 + 2 * i + s)
                    split_lo(((base + s) % 2, i + (base + s + 2) // 2))
            for u in (base + 8, base + 9):
                dve.wait_ge(unit_done, u + 1)
                split_lo(u + 2)
            for j in range(8):
                if j < 7:
                    dve.wait_ge(down_done, 7 * l + j + 1)
                else:
                    dve.wait_ge(unit_done, base + 11)
                dve.scalar_tensor_tensor(x[:, j], PS[:, j, :], gres[:, j:j + 1], x[:, j], ALU.mult, ALU.add).then_inc(x_upd, 1)
            split_lo(base + 12)

        def modulation(gname, vs):
            dve.wait_ge(fin_dve, vs + 2)
            own(dve.tensor_scalar(gs4[:], mod[:, 8 * vs + 8:8 * vs + 16], 1.0, HS, ALU.add, ALU.mult))
            own.wait()
            own(dve.tensor_tensor(gs4[:], gs4[:], pc(gname), ALU.mult))
            dve.tensor_scalar(sh4[:], mod[:, 8 * vs:8 * vs + 8], HS, None, ALU.mult).then_inc(gs_ready, 1)
            own.wait()

        def norm(n, gname, vs):
            dve.wait_ge(sq_used, 8 * n + 8)
            dve.tensor_scalar(ss[:], PS[:, ss_bank(n), 0:4], 1.0 / D, EPS, ALU.mult, ALU.add).then_inc(ss_dve, 1)
            if vs is not None:
                modulation(gname, vs)
            dve.wait_ge(ss_act, n + 1)
            own(dve.reciprocal(rs[:], ss[:]))
            own.wait()
            for m in range(NT):
                dve.tensor_scalar(dg[:, m], ident[:], rs[:, m:m + 1], None, ALU.mult).then_inc(dg_ready, 1)
            dve.wait_ge(rb_pe, n + 1)
            dve.tensor_copy(rstd[:], PS[:, 5, :]).then_inc(rstd_ready, 1)
            dve.wait_ge(rstd_ready, n + 1)

        def norm_apply(n):
            for j in range(9):
                if j < 8:
                    if 8 * n + j >= 2:
                        dve.wait_ge(h_hi, 8 * n + j - 1)
                    dve.tensor_tensor(tn[:, j % 2], x[:, j], rstd[:], ALU.mult).then_inc(tn_ready, 1)
                if j:
                    dve.wait_ge(h_hi, 8 * n + j)
                    dve.tensor_tensor(hl[:, j - 1], h4[:, (j - 1) % 2], hh[:, j - 1], ALU.subtract).then_inc(h_lo, 1)

        def angles():
            C1 = 6.28125
            C2 = float(np.float32(2 * math.pi - C1))
            C3 = float(np.float32(2 * math.pi - C1 - C2))
            PI = float(np.nextafter(np.float32(math.pi), np.float32(0)))
            dve.wait_ge(pos_in, 16)
            own(dve.tensor_copy(xr[:, 0], posi[:]))
            own.wait()
            own(dve.tensor_scalar(xr[:, 0], xr[:, 0], pc("invf"), None, ALU.mult))
            own.wait()
            own(dve.tensor_scalar(xr[:, 2], xr[:, 0], 1.0 / (2 * math.pi), MAGIC, ALU.mult, ALU.add))
            own.wait()
            own(dve.tensor_scalar(xr[:, 2], xr[:, 2], -MAGIC, None, ALU.add))
            own.wait()
            for c in (C1, C2, C3):
                own(dve.scalar_tensor_tensor(xr[:, 0], xr[:, 2], -c, xr[:, 0], ALU.mult, ALU.add))
                own.wait()
            own(dve.tensor_scalar(xr[:, 1], xr[:, 0], math.pi / 2, None, ALU.add))
            own.wait()
            own(dve.tensor_scalar(xr[:, 3], xr[:, 1], math.pi, -2 * math.pi, ALU.is_gt, ALU.mult))
            dve.tensor_scalar(xr[:, 0], xr[:, 0], PI, -PI, ALU.min, ALU.max).then_inc(rope_arg, 1)
            own.wait()
            own(dve.tensor_tensor(xr[:, 1], xr[:, 1], xr[:, 3], ALU.add))
            own.wait()
            dve.tensor_scalar(xr[:, 1], xr[:, 1], PI, -PI, ALU.min, ALU.max).then_inc(rope_arg, 1)

        def even_constants():
            dve.wait_ge(mats_in, 16)
            dve.tensor_copy(identb[:], pm("ident")).then_inc(const_ready, 1)
            dve.tensor_copy(causb[:], pm("causal")).then_inc(const_ready, 1)
            for g in range(NH):
                dve.tensor_tensor(pm("ws", P * g, P), pm("ws", P * g, P), pm("upper"), ALU.mult).then_inc(const_ready, 1)
            for t in (hidc[:, :, :, :, NCMP:NCMP + 1], kcmp[:], vcmp[:]):
                dve.memset(t, 0.0).then_inc(const_ready, 1)
            dve.wait_ge(wg_hi, 1)
            dve.scalar_tensor_tensor(wgl[:].rearrange("p k n -> p (k n)"), pm("wg"), WS, wgh[:].rearrange("p k n -> p (k n)"),
                                     ALU.mult, ALU.subtract).then_inc(const_ready, 1)

        dve.memset(ones[:], 1.0).then_inc(const_ready, 1)
        dve.wait_ge(cols_in, 16)
        dve.wait_ge(cond_ready, 1)
        for n in range(16):
            k, v = n % 8, n // 8
            dve.wait_ge(ada_ready[n % 4], 16 * (n // 4 + 1))
            if k == 0:
                dve.tensor_scalar(adacc[:, v], adab[:, n % 4], cond[:, k:k + 1], None, ALU.mult).then_inc(ada_read, 1)
            else:
                dve.wait_ge(ada_read, n)
                dve.scalar_tensor_tensor(adacc[:, v], adab[:, n % 4], cond[:, k:k + 1], adacc[:, v], ALU.mult, ALU.add)\
                    .then_inc(ada_read, 1)
            if n == 7:
                dve.wait_ge(ident_in, 16)
                own(dve.tensor_copy(ident[:], pm("ident")))
                own.wait()
                norm(0, None, None)
        fin(0)
        split_lo(0)
        fin(1)
        modulation("n1g0", 0)
        for j in range(8):
            dve.wait_ge(h_hi, j + 1)
            dve.tensor_tensor(hl[:, j], h4[:, j % 2], hh[:, j], ALU.subtract).then_inc(h_lo, 1)
            if j == 3:
                split_lo(1)
        even_constants()
        angles()

        def rope(r):
            dst = ksw[:, r] if r < 2 else q[:, r - 2]
            if r == 0:
                dve.wait_ge(rope_tab, 2)
            dve.wait_ge(swap_done, r + 1)
            own(dve.tensor_tensor(rt[:, 0], PS[:, 4 + r % 2, :], sinT[:], ALU.mult))
            own(dve.tensor_tensor(rt[:, 1], xr[:, r % 4], cosT[:], ALU.mult))
            own.wait()
            dve.tensor_tensor(dst, rt[:, 0], rt[:, 1], ALU.add).then_inc(rope_done, 1)
            dve.wait_ge(rope_done, r + 1)

        def lo_g(c):
            dve.wait_ge(g_hi, c + 1)
            dve.tensor_tensor(gcl[:, c].rearrange("p l h n -> p (l h n)"), kcG[:].rearrange("p l h n -> p (l h n)"),
                              gch[:, c].rearrange("p l h n -> p (l h n)"), ALU.subtract).then_inc(g_lo, 1)

        def build(c):
            dve.wait_ge(kc_shift, 32)
            if c:
                dve.wait_ge(g_lo, 1)
            for h in range(2):
                for half in range(2):
                    src = kcS[:, c, h, 1:T + 1].rearrange("p (n l e) -> p l e n", l=8, e=2)[:, :, 0, half:half + NCMP]
                    pe = pc("pev" if c else "pek", 8 * half, 8).unsqueeze(2).to_broadcast([P, 8, NCMP])
                    ins = dve.tensor_tensor(kcG[:, 8 * half:8 * half + 8, h, :], src, pe, ALU.add)
                    if (h, half) == (1, 1):
                        ins.then_inc(g_built, 1)

        gvg = gv[:].rearrange("p m (g d) -> p (m g) d", d=HD)

        def g_norm(step):
            grb = gr[:].unsqueeze(2).to_broadcast([P, 32, HD])
            if step == 0:
                dve.wait_ge(gv_ready, 4)
                own(dve.tensor_reduce(gr[:], gvg, X, ALU.add))
                own.wait()
                own(dve.tensor_scalar(gr[:], gr[:], 1.0 / HD, None, ALU.mult))
            if step == 1:
                own.wait()
                own(dve.tensor_tensor(gvg, gvg, grb, ALU.subtract))
            if step in (2, 3):
                m = 2 * (step - 2)
                own.wait()
                own(dve.tensor_tensor(gsq[step - 2][:], gv[:, m:m + 2], gv[:, m:m + 2], ALU.mult))
                own.wait()
                own(dve.tensor_reduce(gr[:, 8 * m:8 * m + 16], gsq[step - 2][:].rearrange("p m (g d) -> p (m g) d", d=HD), X, ALU.add))
                if step == 3:
                    own.wait()
                    dve.tensor_scalar(gr[:], gr[:], 1.0 / HD, EPS, ALU.mult, ALU.add).then_inc(gvar_ready, 1)
            if step == 4:
                dve.wait_ge(gstd_ready, 1)
                own(dve.reciprocal(gr[:], gm[:]))
                own.wait()
                own(dve.tensor_tensor(gvg, gvg, grb, ALU.mult))
            if step == 5:
                own.wait()
                own(dve.tensor_tensor(gv[:], gv[:], pm("gln", 0, 512).unsqueeze(1).to_broadcast([P, NT, T]), ALU.mult))
            if step == 6:
                own.wait()
                dve.tensor_tensor(gv[:], gv[:], pm("gln", 512, 512).unsqueeze(1).to_broadcast([P, NT, T]), ALU.add).then_inc(gn_ready, 1)

        def g_gate(j):
            dve.wait_ge(gmix_pe, j + 1)
            if j >= 2:
                dve.wait_ge(y_hi, j)
            own(dve.tensor_tensor(yt[:, j % 2].rearrange("p (c t) -> p c t", c=NT),
                                  PS[:, 7, :].rearrange("p (c t) -> p c t", c=NT),
                                  pm("bs", P * j, P).unsqueeze(1).to_broadcast([P, NT, P]), ALU.add))
            own.wait()
            dve.tensor_tensor(yt[:, j % 2], yt[:, j % 2], gu[:, j], ALU.mult).then_inc(gmix_t, 1)

        def g_lo_part(j):
            dve.wait_ge(y_hi, j + 2)
            dve.tensor_tensor(hl[:, 4 + j], yt[:, j % 2], hh[:, 4 + j], ALU.subtract).then_inc(y_lo, 1)

        def c_sub_step(i):
            addm = pm("cmpadd", 32 * i, 32).unsqueeze(1).unsqueeze(1).to_broadcast([P, 4, 2, 32])
            dve.wait_ge(c_S, i + 1)
            if i:
                dve.wait_ge(c_exp, i)
            own(dve.tensor_tensor(cs[:].rearrange("p (t h) n -> p t h n", h=2),
                                  PS[:, 4:6, 0:128].rearrange("p h (t n) -> p t h n", t=4), addm, ALU.add))
            own.wait()
            own(dve.tensor_reduce(cm[:], cs[:], X, ALU.max))
            own.wait()
            dve.tensor_tensor(cs[:], cs[:], cm[:].unsqueeze(2).to_broadcast([P, 8, 32]), ALU.subtract).then_inc(c_sub, 1)

        def c_post_step(i):
            okm = pm("cmpok", 32 * i, 32).unsqueeze(1).to_broadcast([P, 8, 32])
            dve.wait_ge(c_exp, i + 1)
            own(dve.tensor_reduce(csum[:, i], cp[:, i % 2], X, ALU.add))
            own.wait()
            dve.tensor_tensor(cp[:, i % 2], cp[:, i % 2], okm, ALU.mult).then_inc(c_P, 1)

        def c_turned(i):
            dve.wait_ge(c_T, i + 1)
            if i:
                dve.wait_ge(c_V, i)
            dve.tensor_copy(ptc[:].rearrange("p a t -> p (a t)"), PS[:, 6, 0:256]).then_inc(c_ev, 1)

        def c_out(i):
            own(dve.reciprocal(rc[:], csum[:, i]))
            own.wait()
            own(dve.tensor_tensor(sc[:], rc[:], gates[:, i, 0:8], ALU.mult))
            own.wait()
            dve.wait_ge(c_V, i + 1)
            dve.tensor_tensor(oacc[:, i].rearrange("p (h d) -> p h d", h=8), PS[:, 7, :].rearrange("p (h d) -> p h d", h=8),
                              sc[:].unsqueeze(2).to_broadcast([P, 8, HD]), ALU.mult).then_inc(c_O, 1)

        for u in range(2):
            dve.wait_ge(unit_done, u + 1)
            split_lo(u + 2)
        dve.wait_ge(unit_done, 3)
        split_lo(4)
        rope(0)
        rope(1)
        build(0)
        dve.wait_ge(unit_done, 4)
        split_lo(5)
        lo_g(0)
        rope(2)
        rope(3)
        build(1)
        dve.wait_ge(unit_done, 5)
        split_lo(6)
        lo_g(1)
        rope(4)
        rope(5)
        fin(2)
        for u in range(5, 10):
            dve.wait_ge(unit_done, u + 1)
            split_lo(u + 2)
        fin(3)
        dve.wait_ge(cmp_swap, 1)
        at = [31 + 16 * n for n in range(NCMP)]
        own(dve.tensor_tensor(kct[:, 0, 0:NCMP], PS[:, 5, 0:NCMP], sinT[:, at[0]:at[-1] + 1:16], ALU.mult))
        own(dve.tensor_tensor(kct[:, 1, 0:NCMP], kcr[:, 0:NCMP], cosT[:, at[0]:at[-1] + 1:16], ALU.mult))
        own.wait()
        dve.tensor_tensor(kcmp[:, 0:NCMP], kct[:, 0, 0:NCMP], kct[:, 1, 0:NCMP], ALU.add).then_inc(cmp_dve, 1)
        c_sub_step(0)
        c_post_step(0)
        c_turned(0)
        c_sub_step(1)
        c_post_step(1)
        split_lo(U_GU + 1)
        c_out(0)
        c_turned(1)
        c_sub_step(2)
        c_post_step(2)
        c_out(1)
        c_turned(2)
        c_sub_step(3)
        c_post_step(3)
        c_out(2)
        c_turned(3)

        def amax(g):
            i = query_tile(g)
            dve.wait_ge(a_S, g + 1)
            dve.tensor_reduce(nmax[:, g:g + 1], PS[:, (g + 2) % 3, 0:(i + 1) * P], X, ALU.max, negate=True).then_inc(a_max, 1)

        gathered = [0]

        def gather(grp):
            i, b = query_tile(8 * grp), grp % 2
            dve.wait_ge(a_exp, 8 * grp + 8)
            own(dve.reciprocal(rc[:], sums[:, 8 * grp:8 * grp + 8]))
            own.wait()
            own(dve.tensor_tensor(sc[:], rc[:], gates[:, i, 8 * (b + 1):8 * (b + 2)], ALU.mult))
            own.wait()
            dve.wait_ge(a_V, 8 * grp + 8)
            own(dve.tensor_tensor(ot, PS[:, 5 + grp % 2, :].rearrange("p (h d) -> p h d", h=8),
                                  sc[:].unsqueeze(2).to_broadcast([P, 8, HD]), ALU.mult))
            gathered[0] = own.n

        def gather_add(grp):
            i = query_tile(8 * grp)
            dve.wait_ge(dve_own, gathered[0])
            dve.tensor_tensor(oacc[:, i], oacc[:, i], work[:, 5], ALU.add).then_inc(a_O, 1)

        def o_lo(n):
            i = NT - 1 - n
            dve.wait_ge(y_hi, 4 + n + 1 if n else 1)
            dve.tensor_tensor(hl[:, 0:4, i * P:(i + 1) * P], PS[:, 7, :].rearrange("p (f t) -> p f t", f=4),
                              hh[:, 0:4, i * P:(i + 1) * P], ALU.subtract).then_inc(y_lo, 1)

        amax(0)
        g_norm(0)
        amax(1)
        c_out(3)
        for g in range(64):
            i = query_tile(g)
            if g + 2 < 64:
                amax(g + 2)
            if 0 <= g - 5 - G_SPLIT < 8:
                split_lo(U_OUT0 + (g - 5 - G_SPLIT) // 4, (g - 5 - G_SPLIT) % 4)
            if g % 2:
                dve.wait_ge(a_T, g + 1)
                if g >= 2:
                    dve.wait_ge(a_V, g - 1)
                dve.tensor_copy(PTs[:, 1, 0:(i + 1) * P], PS[:, 4, 0:(i + 1) * P]).then_inc(a_evD, 1)
            if g % 8 == 1 and g > 8:
                gather(g // 8 - 1)
            if g % 8 == 3 and g > 8:
                gather_add(g // 8 - 1)
            if g % 16 == 6 and g > 16:
                o_lo(g // 16 - 1)
            if g in G_NORM:
                g_norm(G_NORM[g])
            for j in range(4):
                if g == G_MIX + 3 * j + 1:
                    g_gate(j)
                if g == G_MIX + 3 * j + 3:
                    g_lo_part(j)
            if g - 8 in FIN_AT:
                fin(FIN_AT[g - 8])
        gather(7)
        gather_add(7)
        o_lo(3)
        dve.tensor_scalar(cws[:], pc("cw0"), INV, None, ALU.mult).then_inc(cws_ready, 1)
        out_phase(U_OUT0, 2)
        norm(1, "n2g0", 3)
        norm_apply(1)
        fin(7)
        dve.wait_ge(cws_ready, 1)
        glu_up(0, U_UP0)
        fin(8)
        fin(9)
        glu_down(0, U_DOWN0, 5)
        fin(10)
        fin(11)
        norm(2, "n1g1", 6)
        norm_apply(2)

        dve.wait_ge(mo_in, 64)
        own(dve.tensor_scalar(mus[:, 0], pc("mu"), INV, None, ALU.mult))
        own.wait()
        own(dve.tensor_scalar(mus[:, 1], mus[:, 0], -1.0, INV, ALU.mult, ALU.add))
        own(dve.tensor_scalar(lcs[:], pc("lcw"), INV, None, ALU.mult))
        own(dve.tensor_scalar(oal[:], pc("alpha"), -1.0, 1.0, ALU.mult, ALU.add))
        own(dve.memset(resetm[:], 1.0))
        own.wait()
        dve.wait_ge(spl_ready, 1)
        own(dve.tensor_scalar(spl[:, 1], pc("lam"), -1.0, 0.0, ALU.mult, ALU.max))
        own.wait()
        own(dve.tensor_tensor(spl[:, 1], spl[:, 1], spl[:, 0], ALU.add))
        own.wait()
        own(dve.tensor_scalar(spl[:, 2], spl[:, 1], 8.0, None, ALU.mult))
        own(dve.tensor_scalar(spl[:, 1], spl[:, 1], -8.0, None, ALU.mult))
        own.wait()
        OD.hit(dve.memset(resetm[:, 0:T:P], 0.0), "shift_par")

        for i in range(2):
            for tap in range(2, -1, -1):
                for c in range(2):
                    j = 2 * i + c
                    d = 3 - tap
                    if tap == 2:
                        dve.wait_ge(o_in, j + 1)
                    else:
                        dve.wait_ge(o_sh, 6 * i + 2 * (2 - tap) + c - 1)
                    dve.scalar_tensor_tensor(xc[:, j, d:T], PS[:, 2 * (i % 2) + c, 0:T - d], lcs[:, 4 * tap + j:4 * tap + j + 1],
                                             xc[:, j, d:T], ALU.mult, ALU.add).then_inc(o_sh, 1)
            split_lo(U_IN1 + i + 2)
        for i in (2, 3):
            dve.wait_ge(unit_done, U_IN1 + i + 1)
            split_lo(U_IN1 + i + 2)

        def shifted(i, dst, m):
            for c in range(2):
                dve.wait_ge(o_in, 4 + 2 * (i - 4) + c + 1)
                dve.scalar_tensor_tensor(dst[:, c, 1:T], PS[:, 2 * (i % 2) + c, 0:T - 1], mus[:, 0, m + c:m + c + 1],
                                         dst[:, c, 1:T], ALU.mult, ALU.add).then_inc(o_sh, 1)
            dve.wait_ge(o_sh, 12 + 2 * (i - 3))
            if i < 10:
                split_lo(U_IN1 + i + 2)

        shifted(4, lt, 12)
        OA.wait(dve, "lru_t")
        own(dve.tensor_tensor(ii, ii, xc, ALU.mult))
        own.wait()
        own(dve.tensor_tensor(xc, aa, aa, ALU.mult))
        own.wait()
        OD.hit(dve.scalar_tensor_tensor(rr, xc, 1.0, rr, ALU.add, ALU.mult), "lru_b")
        shifted(5, k_[:, 0:2], 4)
        shifted(6, k_[:, 2:4], 6)
        for j in pairs:
            own(dve.tensor_scalar(kap[:, j], k_[:, j], pc("xi", j, 1), None, ALU.mult))
        own.wait()
        OD.hit(dve.tensor_tensor(sqk, kap[:], kap[:], ALU.mult), "kap")
        OA.wait(dve, "lru_s")
        own(dve.tensor_tensor(ii, ii, rr, ALU.mult))
        own.wait()
        for j in pairs:
            own(dve.tensor_tensor_scan(xc[:, j], aa[:, j], ii[:, j], 0.0, ALU.mult, ALU.add))
        own.wait()
        OD.hit(dve.tensor_tensor(xc, xc, gl, ALU.mult), "yd")
        shifted(7, r_[:, 0:2], 0)
        OA.wait(dve, "lw")
        own(dve.tensor_scalar(epp[:], epp[:], -math.exp(-0.5), None, ALU.mult))
        own.wait()
        for j in pairs:
            own(dve.tensor_tensor_scan(ep[:, j], resetm[:], epp[:, j], 0.0, ALU.mult, ALU.add))
        own.wait()
        epc = ep[:].rearrange("p j (c t) -> p (j c) t", t=P)
        OD.hit(dve.tensor_copy(rmid[:].rearrange("p j c -> p (j c)"), epc[:, :, P // 2 - 1]), "cum")
        OD.wait(dve, "cum")
        shifted(8, r_[:, 2:4], 2)
        own(dve.tensor_tensor(epc, epc, rmid[:].rearrange("p j c -> p (j c)").unsqueeze(2).to_broadcast([P, 16, P]), ALU.subtract))
        own.wait()
        own(dve.memset(ec[:], 0.0))
        own.wait()
        OD.hit(dve.tensor_tensor(ec[:, :, 0:3], ep[:].rearrange("p j (c t) -> p j c t", t=P)[:, :, 0:3, P - 1], rmid[:, :, 1:4], ALU.add), "ec")
        OD.hit(dve.tensor_tensor(epp[:], ep[:], epp[:], ALU.subtract), "dd")
        OP.wait(dve, "kk")
        OD.hit(dve.tensor_scalar(rk[:], PS[:, 4, 0:32], EPS, None, ALU.add), "rkv")
        OA.wait(dve, "rks")
        OD.hit(dve.reciprocal(rk[:], rk[:]), "rki")
        OP.wait(dve, "rkT")
        OD.hit(dve.tensor_copy(rkT, PS[0:8, 5, :]), "rkTc")
        for j in pairs:
            OP.wait(dve, ("ksp", j))
            OD.hit(dve.tensor_tensor(kap[:, j], kap[:, j], PS[:, KSP[j], :], ALU.mult), ("ksp", j))
        OD.wait(dve, ("ksp", 3))
        OA.wait(dve, "exp_pp")

        def prep_a(j):
            own(dve.tensor_tensor(epp[:, j], epp[:, j], kap[:, j], ALU.mult))
            own.wait()
            own(dve.scalar_tensor_tensor(kap[:, j], kap[:, j], -1.0, al[:, j], ALU.mult, ALU.mult))
            own.wait()
            own(dve.tensor_tensor(kap[:, j], kap[:, j], em[:, j], ALU.mult))

        def prep_b(j):
            own(dve.tensor_scalar(al[:, j], al[:, j], pc("alpha", j, 1), oal[:, j:j + 1], ALU.mult, ALU.add))
            own.wait()
            own(dve.tensor_tensor(k_[:, j], k_[:, j], al[:, j], ALU.mult))
            own.wait()
            OD.hit(dve.scalar_tensor_tensor(al[:, j], r_[:, j], pc("rho", j, 1), k_[:, j], ALU.mult, ALU.mult), ("brk", j))
            own(dve.tensor_tensor(k_[:, j], k_[:, j], em[:, j], ALU.mult))
            OD.wait(dve, ("brk", j))
            OD.hit(dve.tensor_tensor(r_[:, j], r_[:, j], ep[:, j], ALU.mult), ("prep", j))

        def four(t):
            return t.rearrange("p (c t) -> p c t", c=4)

        def four_of(m):
            return m.unsqueeze(1).to_broadcast([P, 4, P])

        prep_a(0)
        prep_b(0)
        shifted(9, v_[:, 0:2], 8)
        shifted(10, v_[:, 2:4], 10)
        for j in pairs:
            OP.wait(dve, ("bon", j))
            OD.hit(dve.tensor_tensor(al[:, j], PS[:, 7, :], v_[:, j], ALU.mult), ("bon", j))
            OP.wait(dve, ("A", j))
            for h in range(2):
                own(dve.tensor_tensor(four(Xm[:, h]), four(PS[:, 6 + h, :]), mask("m0"), ALU.mult))
            own.wait()
            for h in range(2):
                ins = dve.tensor_tensor(four(Xm[:, h]), four(Xm[:, h]), four_of(ident[:]), ALU.add)
            OD.hit(ins, ("X0", j))
            OA.wait(dve, ("AT", j))
            for h in range(2):
                own(dve.tensor_tensor(four(Zt[:, 2 * j + h]), four(AT[:, h]), mask("m0t"), ALU.mult))
            own.wait()
            for h in range(2):
                ins = dve.tensor_tensor(four(Zt[:, 2 * j + h]), four(Zt[:, 2 * j + h]), four_of(ident[:]), ALU.add)
            OD.hit(ins, ("Z0", j))
            OP.wait(dve, ("KM", j))
            for h in range(2):
                ins = dve.tensor_tensor(four(KM[:, h]), four(PS[:, 6 + h, :]), mask("strict"), ALU.mult)
            OD.hit(ins, ("KM", j))
            for l in range(1, 7):
                for h in range(2):
                    OP.wait(dve, ("Y", j, l, h))
                    OD.hit(dve.tensor_tensor(four(Y1[:, h]), four(PS[:, h, :]), mask("level", l - 1), ALU.mult), ("Y", j, l, h))
                if l in (1, 2):
                    name = ("RB", j) if l == 1 else ("RK", j)
                    OP.wait(dve, name)
                    for h in range(2):
                        dst = RBt[:, 2 * j + h] if l == 1 else UG[:, h]
                        ins = dve.tensor_tensor(four(dst), four(PS[:, 6 + h, :]), mask("incl"), ALU.mult)
                    OD.hit(ins, name)
                for h in range(2):
                    OP.wait(dve, ("XZ", j, l, h))
                    if l < 6:
                        own(dve.tensor_tensor(Xm[:, h], Xm[:, h], PS[:, 2 + h, :], ALU.add))
                    OD.hit(dve.tensor_tensor(Zt[:, 2 * j + h], Zt[:, 2 * j + h], PS[:, 4 + h, :], ALU.add), ("XZ", j, l, h))
                if j < 3 and l == 3:
                    prep_a(j + 1)
                if j < 3 and l == 4:
                    prep_b(j + 1)
        OD.hit(dve.memset(Sst[:, 0], 0.0), "S0")
        for c in range(4):
            OP.wait(dve, ("G", c))
            OD.hit(dve.tensor_tensor(UG[:, 1].rearrange("p (h f) -> p h f", h=2), PS[:, 6:8, 0:256],
                                     W1[:, c].rearrange("p (h f) -> p h f", h=2), ALU.add), ("G", c))
            if c < 3:
                OP.wait(dve, ("S", c))
                nxt = Sst[:, (c + 1) % 2]
                own(dve.tensor_tensor(nxt, Sst[:, c % 2], PS[:, 1, 0:256], ALU.add))
                own.wait()
                OD.hit(dve.tensor_tensor(nxt.rearrange("p (j d) -> p j d", j=4), nxt.rearrange("p (j d) -> p j d", j=4),
                                         ec[:, :, c].unsqueeze(2).to_broadcast([P, 4, HD]), ALU.mult), ("S", c))
            OP.wait(dve, ("Yc", c))
            yv = Yl[:, :, c * P:(c + 1) * P]
            OD.hit(dve.tensor_tensor(yv, PS[:, 4 + c % 2, :].rearrange("p (j t) -> p j t", j=4), yv, ALU.add), ("Yc", c))
            own(dve.scalar_tensor_tensor(al[:, c], al[:, c], pc("lnb", c, 1), og[:, c], ALU.add, ALU.mult))
            own.wait()
            own(dve.tensor_scalar(og[:, c], og[:, c], pc("lng", c, 1), None, ALU.mult))
            split_lo(U_OUT1 + 1, c)
        for j in pairs:
            OP.wait(dve, ("mean", j))
            OD.hit(dve.scalar_tensor_tensor(Yl[:, j], PS[:, 4 + j, :], -1.0 / HD, Yl[:, j], ALU.mult, ALU.add), ("cen", j))
        OP.wait(dve, "var")
        OD.hit(dve.tensor_scalar(rk[:], PS[:, 0, 0:32], 1.0 / HD, EPS, ALU.mult, ALU.add), "rkv2")
        OA.wait(dve, "rks2")
        OD.hit(dve.reciprocal(rk[:], rk[:]), "rki2")
        OP.wait(dve, "vT")
        OD.hit(dve.tensor_copy(rkT, PS[0:8, 1, :]), "rkT2")
        for j in pairs:
            OP.wait(dve, ("vsp", j))
            own(dve.tensor_tensor(Yl[:, j], Yl[:, j], PS[:, 4 + j, :], ALU.mult))
            own.wait()
            own(dve.tensor_tensor(Yl[:, j], Yl[:, j], og[:, j], ALU.mult))
            own.wait()
            OD.hit(dve.tensor_tensor(Yl[:, j], Yl[:, j], al[:, j], ALU.add), ("y", j))
            for i in ([j - 1] if 0 < j < 3 else [2, 3] if j == 3 else []):
                OA.wait(dve, ("y", i))
                dve.tensor_tensor(hl[:, i], Yl[:, i], hh[:, i], ALU.subtract).then_inc(y_lo, 1)
        dve.tensor_scalar(cws[:], pc("cw1"), INV, None, ALU.mult).then_inc(cws_ready, 1)
        out_phase(U_OUT1, 8)
        norm(3, "n2g1", 9)
        norm_apply(3)
        dve.wait_ge(cws_ready, 2)
        glu_up(1, U_UP1)
        glu_down(1, U_DOWN1, 11)
        norm(4, None, None)
        for j in range(8):
            if j >= 2:
                dve.wait_ge(h_hi, 31 + j)
            dve.tensor_tensor(tn[:, j % 2], x[:, j], rstd[:], ALU.mult).then_inc(tn_ready, 1)

    @block.tensor
    def _(pe):
        def mm3(o, wh, wl, xh, xl, start, stop):
            pe.matmul(o, wh, xh, start=start, stop=False)
            pe.matmul(o, wh, xl, start=False, stop=False)
            return pe.matmul(o, wl, xh, start=False, stop=stop)

        def fin(v, tiles=range(8)):
            if v < 2:
                pe.wait_ge(ada_read, 8 * v + 8)
            else:
                pe.wait_ge(ada_done, v - 1)
            if v and fin_bank(v) == fin_bank(v - 1):
                pe.wait_ge(fin_dve, v)
            for f in tiles:
                ins = pe.matmul(PS[:, fin_bank(v), f:f + 1], adacc[:, v % 2, f * P:(f + 1) * P], ones[:, 0:1], start=True, stop=True)
            if f == 7:
                ins.then_inc(fin_pe, 1)

        def sumsq(n, j):
            pe.wait_ge(sq_ready, 8 * n + j + 1)
            for m in range(NT):
                ins = pe.matmul(PS[:, ss_bank(n), m:m + 1], sq[:, j % 2, m * P:(m + 1) * P], ones[:, 0:1],
                                start=(j == 0 and m == 0), stop=(j == 7), skip_group_check=True)
            ins.then_inc(sq_used, 1)

        def spread(n):
            for m in range(NT):
                pe.wait_ge(dg_ready, 4 * n + m + 1)
                ins = pe.matmul(PS[:, 5, m * P:(m + 1) * P], ones[:], dg[:, m], start=True, stop=True)
            ins.then_inc(rb_pe, 1)

        def fm_unit(u, ready=None, ks=range(8), first=0, last=7):
            s = u[0] if isinstance(u, tuple) else u % 2
            pe.wait_ge(w_lo, (u[1] if isinstance(u, tuple) else u) + 1)
            for k in ks:
                if ready is not None and k < ready[2]:
                    pe.wait_ge(ready[0], ready[1] + k + 1)
                for c in range(2):
                    w = slice(k * 256 + c * P, k * 256 + c * P + P)
                    ins = mm3(PS[:, 2 * s + c, :], whi[:, s, w], wlo[:, s, w], hh[:, k], hl[:, k], k == first, k == last)
            if k == last:
                ins.then_inc(unit_done, 1)

        def tm_unit(u, ms=range(NT)):
            s = u % 2
            pe.wait_ge(w_lo, u + 1)
            for m in ms:
                o = PS[:, 2 * s + m // 2, 256 * (m % 2):256 * (m % 2) + 256]
                t = slice(m * P, (m + 1) * P)
                for k in range(8):
                    w = slice(k * 256, k * 256 + 256)
                    ins = mm3(o, hh[:, k, t], hl[:, k, t], whi[:, s, w], wlo[:, s, w], k == 0, k == 7)
            if m == NT - 1:
                ins.then_inc(unit_done, 1)

        def swap(r):
            pe.wait_ge(xr_ready, r + 1)
            if r >= 2:
                pe.wait_ge(rope_done, r - 1)
            pe.matmul(PS[:, 4 + r % 2, :], pm("swap"), xr[:, r % 4], start=True, stop=True).then_inc(swap_done, 1)

        def out_phase(n, base, y, half_done=False):
            for i in range(4):
                if i == 0 and half_done:
                    fm_unit(base, (y_lo, y, 4), range(4), None, 3)
                else:
                    fm_unit(base + i, (y_lo, y, 4) if i == 0 else None)
                if i:
                    sumsq(n, 2 * i - 2)
                    sumsq(n, 2 * i - 1)
            sumsq(n, 6)
            sumsq(n, 7)
            spread(n)

        def glu_up(n, base):
            fm_unit(base, (h_lo, 8 * n, 8))
            fm_unit(base + 1)
            with pe.Fori(1, NF // 2) as i:
                for s in range(2):
                    fm_unit(((base + s) % 2, base + s + 2 * i))

        def glu_down(l, n, base):
            def unit(s, u, k, start=False, stop=False):
                pe.wait_ge(w_lo, u + 1)
                pe.wait_ge(hid_lo, NF * l + k + 2)
                for kk, j in ([(kk, j) for j in (4, 5, 6, 7, 0, 1, 2, 3) for kk in range(2)] if start else
                              [(kk, j) for kk in range(2) for j in range(8)]):
                    if start and (kk, j) == (0, 0):
                        pe.wait_ge(tap_done, 2 * NF * (l + 1))
                    if start and l == 0 and (kk, j) == (0, 6):
                        pe.wait_ge(fin_dve, 10)
                    w = slice(kk * D + j * P, kk * D + j * P + P)
                    xh = hidh[:, bass.ds(k + kk, 1), :].rearrange("p o t -> p (o t)")
                    xl = hidl[:, bass.ds(k + kk, 1), :].rearrange("p o t -> p (o t)")
                    ins = mm3(PS[:, j, :], whi[:, s, w], wlo[:, s, w], xh, xl, start and kk == 0, stop and kk == 1)
                    if stop and kk == 1 and j < 7:
                        ins.then_inc(down_done, 1)
                ins.then_inc(unit_done, 1)

            unit(base % 2, base, 0, start=True)
            with pe.Fori(0, 4) as i:
                for s in (1, 2):
                    unit((base + s) % 2, base + s + 2 * i, 2 * s + 4 * i)
            unit((base + 9) % 2, base + 9, 18)
            unit((base + 10) % 2, base + 10, 20, stop=True)
            for j in range(8):
                sumsq(n, j)
            if l == 0:
                fin(10)
                fin(11)
            spread(n)

        pe.wait_ge(const_ready, 1)
        for j in range(8):
            sumsq(0, j)
        spread(0)
        fin(0)
        fin(1)
        fm_unit(0, (h_lo, 0, 8))
        fm_unit(1)
        fm_unit(2)
        swap(0)
        swap(1)
        fm_unit(3)
        swap(2)
        swap(3)
        tm_unit(U_V)
        pe.wait_ge(const_ready, 15)
        for m in range(NT):
            for k in range(8):
                t = slice(m * P, (m + 1) * P)
                ins = mm3(PS[:, 6, 24 * m:24 * m + 24], hh[:, k, t], hl[:, k, t], wgh[:, k], wgl[:, k], k == 0, k == 7)
        ins.then_inc(gate_pe, 1)
        fin(2)
        swap(4)
        swap(5)
        for c in range(2):
            pe.wait_ge(g_lo, c + 1)
            if c:
                pe.wait_ge(rope_done, 6)
            for e in range(2):
                u = U_W1 + 2 * c + e
                s = u % 2
                pe.wait_ge(w_lo, u + 1)
                for k in range(8):
                    for ct in range(2):
                        w = slice(k * 256 + ct * P, k * 256 + ct * P + P)
                        ins = mm3(PS[:, 2 + 2 * c + ct, 0:62], whi[:, s, w], wlo[:, s, w],
                                  gch[:, c, 8 * e + k].rearrange("p h n -> p (h n)"),
                                  gcl[:, c, 8 * e + k].rearrange("p h n -> p (h n)"), e == 0 and k == 0, e == 1 and k == 7)
                ins.then_inc(unit_done, 1)
        tm_unit(U_GV, (0, 1))
        fin(3)
        pe.wait_ge(hid_ready, 4)
        pe.wait_ge(v_evac, 3)
        for h in range(2):
            for ct in range(2):
                pe.matmul(PS[64 * h:64 * h + 64, 4, 0:32], pm("w2k", 64 * ct, 64), hidc[:, 0, ct, h, :], start=(ct == 0), stop=(ct == 1))
        for s4 in range(4):
            for ct in range(2):
                ins = pe.matmul(PS[32 * s4:32 * s4 + 32, 6, 0:HD], hidc[:, 1, ct, s4 % 2, :], pm("w2v", 64 * ct, 64),
                                start=(ct == 0), stop=(ct == 1))
        ins.then_inc(cmp_pe, 1)
        tm_unit(U_GV, (2, 3))
        pe.wait_ge(cmp_act, 1)
        pe.matmul(PS[:, 5, 0:32], pm("swap"), kcr[:], start=True, stop=True).then_inc(cmp_swap, 1)
        tm_unit(U_GV + 1, (0, 1))

        def c_scores(i):
            if i:
                pe.wait_ge(c_sub, i)
            else:
                pe.wait_ge(cmp_act, 5)
                pe.wait_ge(cmp_dve, 1)
            for p in range(8):
                h = p % 2
                ins = pe.matmul(PS[:, 4 + h, 32 * (p // 2):32 * (p // 2) + 32], q[64 * h:64 * h + 64, p // 2, i * P:(i + 1) * P],
                                kcmp[64 * h:64 * h + 64, :], start=True, stop=True)
            ins.then_inc(c_S, 1)

        def c_turn(i):
            pe.wait_ge(c_P, i + 1)
            if i:
                pe.wait_ge(c_ev, i)
            for a in range(2):
                ins = pe.transpose(PS[:, 6, a * P:(a + 1) * P], cp[:, i % 2, 4 * a:4 * a + 4].rearrange("p h n -> p (h n)"), ident[:])
            ins.then_inc(c_T, 1)

        def c_values(i):
            pe.wait_ge(c_ev, i + 1)
            if i:
                pe.wait_ge(c_O, i)
            else:
                pe.wait_ge(fin_dve, 4)
            for a in range(2):
                ins = pe.matmul(PS[:, 7, 256 * a:256 * a + 256], ptc[:, a, :], vcmp[:].rearrange("p s d -> p (s d)"),
                                start=True, stop=True)
            ins.then_inc(c_V, 1)

        def scores(g):
            i, b, p = query_tile(g), g // 8 % 2, g % 8
            h, w = p % 2, (i + 1) * P
            if g < 3:
                pe.wait_ge(gu_ready, 2 + g)
            else:
                pe.wait_ge(a_exp, g - 2)
            pe.matmul(PS[:, (g + 2) % 3, 0:w], q[64 * h:64 * h + 64, p // 2, i * P:(i + 1) * P], ksw[64 * h:64 * h + 64, b, 0:w],
                      start=True, stop=False)
            pe.matmul(PS[:, (g + 2) % 3, i * P:w], identb[:], causb[:], start=False, stop=True).then_inc(a_S, 1)

        c_scores(0)
        tm_unit(U_GV + 1, (2, 3))
        c_turn(0)
        c_scores(1)
        fm_unit(U_GU, ks=range(4))
        c_values(0)
        c_turn(1)
        c_scores(2)
        fm_unit(U_GU, ks=range(4, 8))
        c_values(1)
        c_turn(2)
        c_scores(3)
        fm_unit(U_GU + 1, ks=range(4))
        c_values(2)
        c_turn(3)
        scores(0)
        fm_unit(U_GU + 1, ks=range(4, 8))
        c_values(3)

        def g_mix(j):
            if j == 0:
                pe.wait_ge(gn_ready, 1)
                pe.wait_ge(y_lo, 1)
            else:
                pe.wait_ge(gmix_t, j)
            for c in range(NT):
                for h in range(2):
                    ins = pe.matmul(PS[64 * h:64 * h + 64, 7, c * P:(c + 1) * P], gv[:, c, (2 * j + h) * HD:(2 * j + h + 1) * HD],
                                    pm("ws", P * (2 * j + h), P), start=True, stop=True)
            ins.then_inc(gmix_pe, 1)

        def turn(g):
            i = query_tile(g)
            pe.wait_ge(a_exp, g + 1)
            if g >= 2:
                pe.wait_ge(a_evD if g % 2 else a_evA, g // 2)
            for j in range(i + 1):
                ins = pe.transpose(PS[:, 3 + g % 2, j * P:(j + 1) * P], Pb[:, g % 3, j * P:(j + 1) * P], ident[:])
            ins.then_inc(a_T, 1)

        def values(g):
            i, b, p = query_tile(g), g // 8 % 2, g % 8
            grp = g // 8
            pe.wait_ge(a_evD if g % 2 else a_evA, g // 2 + 1)
            if p == 0 and grp >= 2:
                pe.wait_ge(a_O, grp - 1)
            v0 = 128 * b + 64 * (p % 2)
            for j in range(i + 1):
                ins = pe.matmul(PS[:, 5 + grp % 2, HD * p:HD * (p + 1)], PTs[:, g % 2, j * P:(j + 1) * P], vsw[:, j, v0:v0 + HD],
                                start=(j == 0), stop=(j == i))
            ins.then_inc(a_V, 1)

        def turn_out(n):
            i = NT - 1 - n
            pe.wait_ge(a_O, 2 * n + 2)
            if n:
                pe.wait_ge(y_lo, 4 + n)
            pe.wait_ge(fin_dve, (6, 6, 7, 7)[n])
            for f in range(4):
                ins = pe.transpose(PS[:, 7, f * P:(f + 1) * P], oacc[:, i, f * P:(f + 1) * P], ident[:])
            ins.then_inc(o_T, 1)

        def bank7_read(g):
            if g < G_MIX:
                pe.wait_ge(c_O, 4)
            else:
                pe.wait_ge(y_lo, 6)

        pe.wait_ge(c_sub, 4)
        pe.wait_ge(c_ev, 4)
        scores(1)
        for g in range(64):
            if g + 2 < 64:
                scores(g + 2)
            turn(g)
            if g:
                values(g - 1)
            if g % 16 == 5 and g > 16:
                turn_out(g // 16 - 1)
            for j in range(4):
                if g == G_MIX + 3 * j:
                    g_mix(j)
            for first, v in FIN_AT.items():
                if first <= g < first + 8:
                    if g == first:
                        bank7_read(g)
                    fin(v, (g - first,))
        values(63)
        turn_out(3)
        pe.wait_ge(y_lo, 8)
        out_phase(1, U_OUT0, 4)
        fin(7)
        glu_up(1, U_UP0)
        fin(8)
        fin(9)
        glu_down(0, 2, U_DOWN0)

        fm_unit(U_IN1, (h_lo, 16, 8))
        fm_unit(U_IN1 + 1)
        fm_unit(U_IN1 + 2)
        pe.wait_ge(mo_in, 64)

        def four_products(w, x_, name, rows=slice(0, P)):
            at = MATS[w][0] - MAT_LORA
            for j in pairs:
                ins = pe.matmul(PS[:, 4 + j, :], lmat[rows, at + P * j:at + P * j + P], x_(j), start=True, stop=True)
            OP.hit(ins, name)

        pe.wait_ge(o_sh, 12)
        four_products("lwa", lambda j: xc[:, j], "lru_r")
        fm_unit(U_IN1 + 3)
        OA.wait(pe, "lru_r")
        four_products("lwx", lambda j: xc[:, j], "lru_i")
        fm_unit(U_IN1 + 4)
        fm_unit(U_IN1 + 5)
        fm_unit(U_IN1 + 6)
        OA.wait(pe, "lora")
        four_products("wab", lambda j: lt[0:64, 0], "pre_w", slice(0, 64))
        fm_unit(U_IN1 + 7)
        OA.wait(pe, "lw")
        four_products("wab", lambda j: lt[64:128, 0], "pre_a", slice(64, 128))
        fm_unit(U_IN1 + 8)
        OA.wait(pe, "av")
        four_products("gb", lambda j: lt[:, 1], "pre_g")
        fm_unit(U_IN1 + 9, ks=range(4))

        def head_sums(src, bank, name):
            for m in range(NT):
                for j in pairs:
                    ins = pe.matmul(PS[:, bank, 8 * m + 2 * j:8 * m + 2 * j + 2], src[:, j, m * P:(m + 1) * P], po("headcol"),
                                    start=True, stop=True)
            OP.hit(ins, name)

        def turn_sums(bank, name):
            for m in range(NT):
                ins = pe.transpose(PS[0:8, bank, m * P:(m + 1) * P], rk[:, 8 * m:8 * m + 8], ident[:])
            OP.hit(ins, name)

        def spread_heads(j, src, bank, name):
            OP.hit(pe.matmul(PS[:, bank, :], sel8[:, P * j:P * j + P], src, start=True, stop=True), name)

        OD.wait(pe, "kap")
        OA.wait(pe, "g")
        head_sums(sqk, 4, "kk")
        fm_unit(U_IN1 + 9, ks=range(4, 8))
        OD.wait(pe, "rki")
        turn_sums(5, "rkT")
        OD.wait(pe, "rkTc")
        for j in pairs:
            spread_heads(j, rkT, KSP[j], ("ksp", j))
        fm_unit(U_IN1 + 10)

        def products(bank, a, b, j, name):
            for c in range(4):
                for h in range(2):
                    f = slice(HD * h, HD * h + HD)
                    t = slice(c * P, (c + 1) * P)
                    ins = pe.matmul(PS[:, bank + h, t], a[f, j, t], b[f, j, t], start=True, stop=True)
            OP.hit(ins, name)

        def turn_tile(bank, src, j, name):
            for c in range(4):
                ins = pe.transpose(PS[:, bank, c * P:(c + 1) * P], src[:, j, c * P:(c + 1) * P], ident[:])
            OP.hit(ins, name)

        def by_chunk(bank, lhs, rhs):
            for c in range(4):
                t = slice(c * P, (c + 1) * P)
                ins = pe.matmul(PS[:, bank, t], lhs[:, t], rhs[:, t], start=True, stop=True)
            return ins

        def between(j, l):
            if l == 1:
                OD.wait(pe, ("KM", j))
                products(6, kap, r_, j, ("RB", j))
            if l == 2:
                OD.wait(pe, ("RB", j))
                products(6, k_, r_, j, ("RK", j))
            if l == 3:
                OD.wait(pe, ("RK", j))
                turn_tile(6, v_, j, ("TV", j))
            if l == 4:
                turn_tile(7, kap, j, ("TB", j))
                OA.wait(pe, ("VT", j))
                turn_tile(6, k_, j, ("TK", j))
            if l == 5:
                OA.wait(pe, ("bT", j))
                for c in range(4):
                    for h in range(2):
                        ins = pe.matmul(PS[:, 7, P * c + HD * h:P * c + HD * h + HD], KM[:, h, c * P:(c + 1) * P],
                                        VT[:, j, P * c + HD * h:P * c + HD * h + HD], start=True, stop=True)
                OP.hit(ins, ("W", j))
            if l == 6:
                OA.wait(pe, ("kT", j))
                for c in range(4):
                    for h in range(2):
                        ins = pe.matmul(PS[HD * h:HD * h + HD, 6, c * P:(c + 1) * P], VT[:, j, P * c + HD * h:P * c + HD * h + HD],
                                        UG[:, h, c * P:(c + 1) * P], start=True, stop=True)
                OP.hit(ins, ("YL", j))

        for j in pairs:
            OD.wait(pe, ("brk", j))
            if j:
                OA.wait(pe, ("W", j - 1))
            OP.hit(pe.matmul(PS[:, 7, :], po("head"), al[:, j], start=True, stop=True), ("bon", j))
            OD.wait(pe, ("prep", j))
            OD.wait(pe, ("bon", j))
            if j:
                OA.wait(pe, ("YL", j - 1))
            products(6, epp, kap, j, ("A", j))
            if j:
                OD.wait(pe, ("XZ", j - 1, 6, 1))
            products(4, kap, epp, j, ("AT", j))
            OD.wait(pe, ("X0", j))
            products(6, k_, epp, j, ("KM", j))
            OD.wait(pe, ("Z0", j))
            for l in range(1, 7):
                for h in range(2):
                    if l > 1:
                        OD.wait(pe, ("XZ", j, l - 1, h))
                    OP.hit(by_chunk(h, AT[:, h], Xm[:, h]), ("Y", j, l, h))
                between(j, l)
                for h in range(2):
                    OD.wait(pe, ("Y", j, l, h))
                    if l < 6:
                        by_chunk(2 + h, Zt[:, 2 * j + h], Y1[:, h])
                    OP.hit(by_chunk(4 + h, Y1[:, h], Zt[:, 2 * j + h]), ("XZ", j, l, h))
        s1 = U_OUT1 % 2
        parts = [(k, c, i) for k in range(4, 8) for c in range(2) for i in range(3)]

        def out_part(a, b):
            for k, c, i in parts[a:b]:
                w = slice(k * 256 + c * P, k * 256 + c * P + P)
                pe.matmul(PS[:, 2 * s1 + c, :], (whi, whi, wlo)[i][:, s1, w], (hh, hl, hh)[i][:, k], start=(k == 4 and i == 0), stop=False)

        pe.wait_ge(ydl_ready, 1)
        pe.wait_ge(w_lo, U_OUT1 + 1)
        OD.wait(pe, "S0")
        OA.wait(pe, ("YL", 3))
        OA.wait(pe, "exp_c")
        for c in range(4):
            t = slice(c * P, (c + 1) * P)
            S = Sst[:, c % 2]
            if c:
                OD.wait(pe, ("S", c - 1))
            for j in pairs:
                for h in range(2):
                    f = slice(HD * h, HD * h + HD)
                    ins = pe.matmul(PS[:, 6 + h, HD * j:HD * j + HD], epp[f, j, t], S[f, HD * j:HD * j + HD], start=True, stop=True)
            OP.hit(ins, ("G", c))
            out_part(6 * c, 6 * c + 3)
            OD.wait(pe, ("G", c))
            for h in range(2):
                for j in pairs:
                    o = slice(256 * h + HD * j, 256 * h + HD * j + HD)
                    ins = pe.matmul(PS[:, 0, o], Zt[:, 2 * j + h, t], UG[:, 1, o], start=True, stop=True)
            OP.hit(ins, ("U", c))
            out_part(6 * c + 3, 6 * c + 6)
            OA.wait(pe, ("U", c))
            if c < 3:
                for j in pairs:
                    for h in range(2):
                        d = slice(P * c + HD * h, P * c + HD * h + HD)
                        o = PS[HD * h:HD * h + HD, 1, HD * j:HD * j + HD]
                        pe.matmul(o, bT[:, j, d], UG[:, 0, 256 * h + HD * j:256 * h + HD * j + HD], start=True, stop=False)
                        ins = pe.matmul(o, kT[:, j, d], VT[:, j, d], start=False, stop=True)
                OP.hit(ins, ("S", c))
            if c >= 2:
                OD.wait(pe, ("Yc", c - 2))
            for j in pairs:
                for h in range(2):
                    f = slice(HD * h, HD * h + HD)
                    o = PS[f, 4 + c % 2, j * P:(j + 1) * P]
                    pe.matmul(o, S[f, HD * j:HD * j + HD], r_[f, j, t], start=True, stop=False)
                    ins = pe.matmul(o, UG[:, 0, 256 * h + HD * j:256 * h + HD * j + HD], RBt[:, 2 * j + h, t], start=False, stop=True)
            OP.hit(ins, ("Yc", c))
        OD.wait(pe, ("Yc", 3))
        for j in pairs:
            OP.hit(pe.matmul(PS[:, 4 + j, :], po("head"), Yl[:, j], start=True, stop=True), ("mean", j))
        for j in pairs:
            OA.wait(pe, ("sq", j))
        head_sums(em, 0, "var")
        OD.wait(pe, "rki2")
        turn_sums(1, "vT")
        OD.wait(pe, "rkT2")
        for j in pairs:
            spread_heads(j, rkT, 4 + j, ("vsp", j))
        out_phase(3, U_OUT1, 8, True)
        glu_up(3, U_UP1)
        glu_down(1, 4, U_DOWN1)

    ctx.close()


def _unit(w):
    return w.reshape(8, P, 256).transpose(1, 0, 2).reshape(P, UNIT)


def _units(w):
    return [_unit(w[:, c:c + 256]) for c in range(0, w.shape[1], 256)]


def layout(inputs):
    a = {k: np.asarray(v) for k, v in inputs.items()}
    f32 = np.float32
    heads = [h for t in range(4) for h in (t, 4 + t)]
    hcols = np.concatenate([np.arange(h * HD, (h + 1) * HD) for h in heads])
    win = a["ev_w_in"][0]
    off = np.cumsum([0, 512] + [128] * 6 + [24, 512, 512])
    seg = [win[:, off[i]:off[i + 1]] for i in range(10)]
    wq, kc, vc, ks, vs, kw, vw, wg, gu, gv = seg
    units = _units(np.concatenate([kc, vc, ks, kw, wq[:, hcols], vs, vw], 1))
    for w1 in (a["nsa_w1_k"][0], a["nsa_w1_v"][0]):
        units += [_unit(w1[:1024]), _unit(w1[1024:])]
    units += _units(np.concatenate([gv, gu], 1))
    wo = a["ev_w_out"][0]
    units += _units(np.concatenate([wo[:512][hcols], wo[512:]], 0))

    def ffn(layer):
        up, down = a["ffn_up"][layer], a["ffn_down"][layer]
        us = [_unit(np.concatenate([up[:, j * P:(j + 1) * P], up[:, FF + j * P:FF + (j + 1) * P]], 1)) for j in range(NF)]
        return us + [down[2 * v * P:(2 * v + 2) * P].reshape(2, P, D).transpose(1, 0, 2).reshape(P, UNIT) for v in range(NF // 2)]

    units += ffn(0)
    od = a["od_w_in"][0]
    order = [od[:, 2304:2816], od[:, 1792:2304], od[:, 1536:1792], od[:, 512:1024], od[:, 0:512], od[:, 1024:1536]]
    units += _units(np.concatenate(order, 1)) + _units(a["od_w_out"][0]) + ffn(1)
    wstream = np.ascontiguousarray(np.stack(units))
    assert wstream.shape == (UNITS, P, UNIT)
    aw = a["ada_w"].reshape(2, 8, P, 6, D).transpose(0, 3, 1, 2, 4).reshape(NV, 8, P, D)
    ada = np.ascontiguousarray(aw.reshape(8 * NV, P, D))

    def feat(v):
        return np.asarray(v).reshape(-1, P).T

    cw = [a["ffn_conv_w"][l].reshape(3, 2 * NF, P).transpose(2, 0, 1).reshape(P, -1) for l in range(2)]
    invf = np.zeros((P, 1), f32)
    f = (THETA ** (-np.arange(0, ROPE, 2, dtype=f32) / ROPE)).astype(f32)
    for h in range(2):
        invf[h * HD:h * HD + 8, 0] = f
        invf[h * HD + 8:h * HD + 16, 0] = f
    cols = {
        "c": feat(a["c"]), "ada_b": feat(a["ada_b"]), "n1g0": feat(a["norm1_g"][0]), "n2g0": feat(a["norm2_g"][0]),
        "n1g1": feat(a["norm1_g"][1]), "n2g1": feat(a["norm2_g"][1]), "fg": feat(a["final_g"]),
        "cw0": cw[0], "cb0": feat(a["ffn_conv_b"][0]), "cw1": cw[1], "cb1": feat(a["ffn_conv_b"][1]),
        "mu": feat(a["rwkv_mu"]), "w0": feat(a["rwkv_w0"]), "a0": feat(a["rwkv_a0"]), "xi": feat(a["rwkv_xi"]),
        "alpha": feat(a["rwkv_alpha"]), "rho": feat(a["rwkv_rho"]), "lng": feat(a["rwkv_ln_g"]), "lnb": feat(a["rwkv_ln_b"]),
        "lcw": feat(a["lru_conv_w"]), "lcb": feat(a["lru_conv_b"]), "ba": feat(a["lru_ba"]), "bx": feat(a["lru_bx"]),
        "lam": feat(a["lru_lambda"]), "pek": feat(a["nsa_pe_k"]), "pev": feat(a["nsa_pe_v"]), "invf": invf,
    }
    pcol = np.ascontiguousarray(np.concatenate([cols[n].reshape(P, COLS[n][1]) for n in COLS], 1))
    r = np.arange(P)
    swap = np.zeros((P, P), f32)
    for h in range(2):
        for i in range(8):
            swap[h * HD + 8 + i, h * HD + i] = -1.0
            swap[h * HD + i, h * HD + 8 + i] = 1.0
    tpos = np.arange(T).reshape(NT, P).T
    ends = np.concatenate([np.arange(NCMP) * 16 + 31, [10 ** 6]])
    ok = (ends[None, None, :] <= tpos[:, :, None]).astype(f32)

    def blockdiag(w):
        o = np.zeros((P, 4, P), f32)
        for n in range(8):
            h = n % 2 * HD
            o[h:h + HD, n // 2, h:h + HD] = w[n]
        return o.reshape(P, 512)

    hcol = (r[:, None] // HD == np.arange(2)[None]).astype(f32)
    sel8 = np.zeros((P, 512), f32)
    for n in range(8):
        sel8[n, n * HD:(n + 1) * HD] = 1.0
    level = [((r[:, None] >> l) % 2 == 1) & ((r[:, None] >> l) - 1 == (r[None] >> l)) for l in range(7)]
    gorder = [heads[p] * 3 + b for b in range(3) for p in range(8)]
    bs = np.repeat(a["gmlp_bs"][0].reshape(4, 2, P).transpose(1, 0, 2), HD, axis=0)
    mats = {
        "ident": np.eye(P, dtype=f32), "swap": swap,
        "causal": np.where(r[None] > r[:, None], NEG, 0).astype(f32), "upper": (r[:, None] <= r[None]).astype(f32),
        "head": (r[:, None] // HD == r[None] // HD).astype(f32),
        "headcol": hcol, "sel8": sel8,
        "cmpadd": np.where(ok > 0, 0, NEG).astype(f32).reshape(P, P), "cmpok": ok.reshape(P, P),
        "wg": wg[:, gorder].reshape(8, P, 24).transpose(1, 0, 2), "w2k": a["nsa_w2_k"][0].reshape(2, P, HD).transpose(1, 0, 2),
        "w2v": a["nsa_w2_v"][0].reshape(2, P, HD).transpose(1, 0, 2),
        "ws": a["gmlp_ws"][0].transpose(2, 0, 1), "bs": bs,
        "gln": np.broadcast_to(np.concatenate([a["gmlp_ln_g"][0].reshape(-1), a["gmlp_ln_b"][0].reshape(-1)]), (P, 1024)),
        "wab": np.concatenate([a["rwkv_wB"][0], a["rwkv_aB"][0]], 0), "gb": a["rwkv_gB"][0],
        "lwa": blockdiag(a["lru_wa"][0]), "lwx": blockdiag(a["lru_wx"][0]),
    }
    pmat = np.ascontiguousarray(np.concatenate([mats[n].reshape(P, MATS[n][1]) for n in MATS], 1))
    pmask = np.stack([level[0], level[0].T, r[:, None] < r[None], r[:, None] <= r[None]] + level[1:], 1)
    pmask = np.ascontiguousarray(pmask.reshape(P, -1).astype(np.float16))
    pos = np.ascontiguousarray(np.broadcast_to(a["positions"].reshape(1, T), (P, T)))
    xT = np.ascontiguousarray(a["x"].reshape(T, KC, P).transpose(2, 1, 0))
    return {"wstream": wstream, "ada": ada, "pcol": pcol, "pmat": pmat, "pmask": pmask, "pos": pos, "xT": xT}


def kernel(**inputs):
    import concourse.bacc as bacc
    from concourse.bass_utils import run_bass_kernel_spmd

    nc = bacc.Bacc("TRN2", target_bir_lowering=False, num_devices=1)
    arrays = layout(inputs)
    args = [nc.dram_tensor(n, v.shape, mybir.dt.from_np(v.dtype), kind="ExternalInput").ap() for n, v in arrays.items()]
    out = nc.dram_tensor("out", [P, KC, T], F32, kind="ExternalOutput").ap()
    program(nc, *args, out)
    r = run_bass_kernel_spmd(nc, [arrays], core_ids=[0])
    y = r.results[0]["out"]
    return np.ascontiguousarray(y.transpose(2, 1, 0)).reshape(1, T, D)
```
